# Optimizing a Trainium2 kernel written in Bass

```python
import math
import jax, jax.numpy as jnp
from jax import lax
import numpy as np
import jax
import jax.numpy as jnp

D_MODEL = 1024
BATCH = 1
SEQ = 512
DEPTH = 1

CHUNK = 64
Q_BLOCK = 128
EPS = 1e-6

DIFF_HEADS = 8
DIFF_DH = 64
DIFF_W = DIFF_HEADS * 2 * DIFF_DH

CH_HEADS = 8
CH_DH = 64
CH_W = CH_HEADS * CH_DH
CH_LEFT = 8
REL_CLIP = 128

PEER_HEADS = 8
PEER_NKEYS = 128
PEER_NEXP = PEER_NKEYS * PEER_NKEYS
PEER_DKEY = 128
PEER_TOPK = 16
PEER_BLOCK = 128

IN_SIZES = (DIFF_W, DIFF_W, DIFF_W, CH_W, CH_W, CH_W, D_MODEL, D_MODEL)
IN_COLS = sum(IN_SIZES)
IN_SPLITS = tuple(int(s) for s in np.cumsum(IN_SIZES)[:-1])


def rmsnorm(x, w):
    xf = x.astype(jnp.float32)
    y = xf * lax.rsqrt(jnp.mean(xf * xf, axis=-1, keepdims=True) + EPS)
    return (y * w.astype(jnp.float32)).astype(x.dtype)

def alibi_slopes(n_heads):
    return jnp.exp2(-8.0 * jnp.arange(1, n_heads + 1, dtype=jnp.float32) / n_heads)

def diff_attention(q, k, v, lq1, lk1, lq2, lk2, subln_w, lam_init):
    B, S = q.shape[0], q.shape[1]
    nqb = S // Q_BLOCK
    f32 = jnp.float32
    lam = (jnp.exp(jnp.sum(lq1.astype(f32) * lk1.astype(f32)))
           - jnp.exp(jnp.sum(lq2.astype(f32) * lk2.astype(f32))) + lam_init)
    k1, k2 = k[..., 0, :], k[..., 1, :]
    qb = jnp.moveaxis(q.reshape(B, nqb, Q_BLOCK, DIFF_HEADS, 2, DIFF_DH), 1, 0)
    slopes = alibi_slopes(DIFF_HEADS)
    kpos = jnp.arange(S, dtype=jnp.int32)
    scale = DIFF_DH ** -0.5

    def block(args):
        qblk, bi = args
        qpos = bi * Q_BLOCK + jnp.arange(Q_BLOCK, dtype=jnp.int32)
        dist = jnp.abs(qpos[:, None] - kpos[None, :]).astype(f32)
        bias = -slopes[:, None, None] * dist
        allowed = (kpos[None, :] // CHUNK) <= (qpos[:, None] // CHUNK)

        def probs(qq, kk):
            s = jnp.einsum('bqhd,bkhd->bhqk', qq, kk).astype(f32) * scale + bias
            return jax.nn.softmax(jnp.where(allowed, s, -jnp.inf), axis=-1)

        a = probs(qblk[..., 0, :], k1) - lam * probs(qblk[..., 1, :], k2)
        return jnp.einsum('bhqk,bkhe->bqhe', a.astype(v.dtype), v)

    o = lax.map(block, (qb, jnp.arange(nqb, dtype=jnp.int32)))
    o = jnp.moveaxis(o, 0, 1).reshape(B, S, DIFF_HEADS, 2 * DIFF_DH)
    o = rmsnorm(o, subln_w) * (1.0 - lam_init)
    return o.reshape(B, S, DIFF_W)

def chunk_attention(q, k, v, rel_table):
    B, S = q.shape[0], q.shape[1]
    nc = S // CHUNK
    band = (CH_LEFT + 1) * CHUNK
    f32 = jnp.float32
    qc = q.reshape(B, nc, CHUNK, CH_HEADS, CH_DH)
    pad = ((0, 0), (CH_LEFT * CHUNK, 0), (0, 0), (0, 0))
    kp = jnp.pad(k, pad).reshape(B, nc + CH_LEFT, CHUNK, CH_HEADS, CH_DH)
    vp = jnp.pad(v, pad).reshape(B, nc + CH_LEFT, CHUNK, CH_HEADS, CH_DH)
    kb = jnp.concatenate([kp[:, j:j + nc] for j in range(CH_LEFT + 1)], axis=2)
    vb = jnp.concatenate([vp[:, j:j + nc] for j in range(CH_LEFT + 1)], axis=2)
    r = jnp.arange(band, dtype=jnp.int32)
    qi = jnp.arange(CHUNK, dtype=jnp.int32)
    rel = qi[:, None] - r[None, :] + CH_LEFT * CHUNK
    bias = rel_table[:, jnp.clip(rel, -REL_CLIP, REL_CLIP) + REL_CLIP].astype(f32)
    valid = (jnp.arange(nc, dtype=jnp.int32)[:, None] * CHUNK - CH_LEFT * CHUNK + r[None, :]) >= 0
    s = jnp.einsum('bcqhd,bckhd->bhcqk', qc, kb).astype(f32) * (CH_DH ** -0.5) + bias[:, None]
    s = jnp.where(valid[:, None, :], s, -jnp.inf)
    p = jax.nn.softmax(s, axis=-1)
    o = jnp.einsum('bhcqk,bckhd->bcqhd', p.astype(v.dtype), vb)
    return o.reshape(B, S, CH_W)

def peer(xn, wq, keys, u, v):
    B, S, D = xn.shape
    xt = xn.reshape(-1, PEER_BLOCK, D)
    f32 = jnp.float32

    def block(xb):
        q = (xb @ wq).reshape(PEER_BLOCK, PEER_HEADS, 2, PEER_DKEY // 2)
        s1 = jnp.einsum('thd,hnd->thn', q[:, :, 0], keys[:, 0]).astype(f32)
        s2 = jnp.einsum('thd,hnd->thn', q[:, :, 1], keys[:, 1]).astype(f32)
        v1, i1 = lax.top_k(s1, PEER_TOPK)
        v2, i2 = lax.top_k(s2, PEER_TOPK)
        cand = (v1[..., :, None] + v2[..., None, :]).reshape(PEER_BLOCK, PEER_HEADS, PEER_TOPK * PEER_TOPK)
        sc, ci = lax.top_k(cand, PEER_TOPK)
        e = (jnp.take_along_axis(i1, ci // PEER_TOPK, axis=-1) * PEER_NKEYS
             + jnp.take_along_axis(i2, ci % PEER_TOPK, axis=-1))
        g = jax.nn.softmax(sc, axis=-1)
        ue = u[e]
        ve = v[e]
        hid = jnp.einsum('thkd,td->thk', ue, xb).astype(f32)
        a = (jax.nn.gelu(hid, approximate=False) * g).astype(xb.dtype)
        return jnp.einsum('thk,thkd->td', a, ve)

    return lax.map(block, xt).reshape(B, S, D)

def first_inputs(seed: int = 0) -> dict:
    key = jax.random.key(seed)
    ks = jax.random.split(key, 20)
    n = jax.random.normal
    f32 = jnp.float32
    L, D = DEPTH, D_MODEL
    return {
        "x": n(ks[0], (BATCH, SEQ, D), f32),
        "norm1_w": 1.0 + 0.02 * n(ks[1], (L, D), f32),
        "w_in": n(ks[2], (L, D, IN_COLS), f32) * D ** -0.5,
        "b_gate": 0.01 * n(ks[3], (L, 2 * D), f32),
        "diff_lq1": 0.1 * n(ks[4], (L, DIFF_DH), f32),
        "diff_lk1": 0.1 * n(ks[5], (L, DIFF_DH), f32),
        "diff_lq2": 0.1 * n(ks[6], (L, DIFF_DH), f32),
        "diff_lk2": 0.1 * n(ks[7], (L, DIFF_DH), f32),
        "diff_subln_w": 1.0 + 0.02 * n(ks[8], (L, 2 * DIFF_DH), f32),
        "chunk_rel_bias": 0.1 * n(ks[9], (L, CH_HEADS, 2 * REL_CLIP + 1), f32),
        "w_branch_diff": n(ks[10], (L, DIFF_W, D), f32) * DIFF_W ** -0.5,
        "w_branch_chunk": n(ks[11], (L, CH_W, D), f32) * CH_W ** -0.5,
        "w_out": n(ks[12], (L, D, D), f32) * D ** -0.5,
        "norm2_w": 1.0 + 0.02 * n(ks[13], (L, D), f32),
        "peer_wq": n(ks[14], (L, D, PEER_HEADS * PEER_DKEY), f32) * D ** -0.5,
        "peer_keys": n(ks[15], (L, PEER_HEADS, 2, PEER_NKEYS, PEER_DKEY // 2), f32) * (PEER_DKEY // 2) ** -0.5,
        "peer_u": n(ks[16], (L, PEER_NEXP, D), f32) * D ** -0.5,
        "peer_v": n(ks[17], (L, PEER_NEXP, D), f32) * D ** -0.5,
        "final_norm_w": 1.0 + 0.02 * n(ks[18], (D,), f32),
    }

def first_block(x, norm1_w, w_in, b_gate, diff_lq1, diff_lk1, diff_lq2, diff_lk2, diff_subln_w,
              chunk_rel_bias, w_branch_diff, w_branch_chunk, w_out, norm2_w, peer_wq, peer_keys,
              peer_u, peer_v, final_norm_w):
    B, S, D = x.shape
    h = x
    for l in range(DEPTH):
        lam_init = 0.8 - 0.6 * math.exp(-0.3 * l)
        xn = rmsnorm(h, norm1_w[l])
        proj = xn @ w_in[l]
        qd, kd, vd, qc, kc, vc, gd, gc = jnp.split(proj, IN_SPLITS, axis=-1)
        o_d = diff_attention(qd.reshape(B, S, DIFF_HEADS, 2, DIFF_DH),
                             kd.reshape(B, S, DIFF_HEADS, 2, DIFF_DH),
                             vd.reshape(B, S, DIFF_HEADS, 2 * DIFF_DH),
                             diff_lq1[l], diff_lk1[l], diff_lq2[l], diff_lk2[l], diff_subln_w[l], lam_init)
        o_c = chunk_attention(qc.reshape(B, S, CH_HEADS, CH_DH), kc.reshape(B, S, CH_HEADS, CH_DH),
                              vc.reshape(B, S, CH_HEADS, CH_DH), chunk_rel_bias[l])
        g_d = jax.nn.sigmoid(gd + b_gate[l, :D])
        g_c = jax.nn.sigmoid(gc + b_gate[l, D:])
        merged = g_d * (o_d @ w_branch_diff[l]) + g_c * (o_c @ w_branch_chunk[l])
        h = h + merged @ w_out[l]
        h = h + peer(rmsnorm(h, norm2_w[l]), peer_wq[l], peer_keys[l], peer_u[l], peer_v[l])
    return rmsnorm(h, final_norm_w)


DEPTH_2 = 2

N_META = 16
N_MIXERS = 3
LEAD_PAD = (-N_META) % CHUNK
RMS_EPS = 1e-6
D_FF = 4 * D_MODEL

GDN_QK_HEADS = 8
GDN_V_HEADS = 16
GDN_HEAD_DIM = 128
GDN_CONV = 4
GDN_QK_DIM = GDN_QK_HEADS * GDN_HEAD_DIM
GDN_V_DIM = GDN_V_HEADS * GDN_HEAD_DIM
GDN_CONV_DIM = 2 * GDN_QK_DIM + GDN_V_DIM
GDN_IN = GDN_CONV_DIM + GDN_V_DIM + 2 * GDN_V_HEADS

MLSTM_HEADS = 8
MLSTM_QK_DIM = D_MODEL // 2
MLSTM_V_DIM = D_MODEL
MLSTM_DQK = MLSTM_QK_DIM // MLSTM_HEADS
MLSTM_DV = MLSTM_V_DIM // MLSTM_HEADS
MLSTM_IN = 2 * MLSTM_QK_DIM + 2 * MLSTM_V_DIM + 2 * MLSTM_HEADS
GATE_SOFTCAP = 15.0

MLA_HEADS = 16
MLA_NOPE = 64
MLA_ROPE = 32
MLA_QK = MLA_NOPE + MLA_ROPE
MLA_V = 64
MLA_Q_RANK = 384
MLA_KV_RANK = 256
MLA_IN = MLA_Q_RANK + MLA_KV_RANK + MLA_ROPE
ROPE_THETA = 10000.0

N_GDN_LAYERS = len(range(0, DEPTH_2, N_MIXERS))
N_MLSTM_LAYERS = len(range(1, DEPTH_2, N_MIXERS))
N_MLA_LAYERS = len(range(2, DEPTH_2, N_MIXERS))


def rms_norm(x, w):
    xf = x.astype(jnp.float32)
    y = xf * lax.rsqrt(jnp.mean(xf * xf, axis=-1, keepdims=True) + RMS_EPS)
    return (y * w.astype(jnp.float32)).astype(x.dtype)

def l2_norm(x):
    xf = x.astype(jnp.float32)
    return xf * lax.rsqrt(jnp.sum(xf * xf, axis=-1, keepdims=True) + RMS_EPS)

def to_chunks(x, pad_value=0.0):
    widths = [(0, 0), (LEAD_PAD, 0)] + [(0, 0)] * (x.ndim - 2)
    x = jnp.pad(x, widths, constant_values=pad_value)
    b, tp = x.shape[:2]
    x = x.reshape((b, tp // CHUNK, CHUNK) + x.shape[2:])
    return jnp.moveaxis(x, 3, 1)

def from_chunks(x):
    b, nh, n, c, d = x.shape
    x = jnp.moveaxis(x, 1, 3).reshape(b, n * c, nh, d)
    return x[:, LEAD_PAD:]

def causal_conv_silu(x, w):
    k, c = w.shape
    y = lax.conv_general_dilated(x, w[:, None, :].astype(x.dtype), window_strides=(1,),
                                 padding=[(k - 1, 0)], dimension_numbers=('NWC', 'WIO', 'NWC'),
                                 feature_group_count=c)
    return jax.nn.silu(y)

def chunk_gated_delta_rule(q, k, v, g, beta):
    q, k, v = to_chunks(q), to_chunks(k), to_chunks(v)
    g, beta = to_chunks(g), to_chunks(beta)
    dv = v.shape[-1]
    causal = jnp.tril(jnp.ones((CHUNK, CHUNK), dtype=bool))
    strict = jnp.tril(jnp.ones((CHUNK, CHUNK), dtype=bool), k=-1)
    cum = jnp.cumsum(g, axis=-1)
    decay = jnp.exp(jnp.where(causal, cum[..., :, None] - cum[..., None, :], -jnp.inf))
    k_beta = k * beta[..., None]
    a = jnp.where(strict, jnp.einsum('bhnid,bhnjd->bhnij', k_beta, k) * decay, 0.0)
    eye = jnp.eye(CHUNK, dtype=a.dtype)
    rhs = jnp.concatenate([v * beta[..., None], k_beta * jnp.exp(cum)[..., None]], axis=-1)
    sol = lax.linalg.triangular_solve(a + eye, rhs, left_side=True, lower=True, unit_diagonal=True)
    u, w = sol[..., :dv], sol[..., dv:]
    attn = jnp.einsum('bhnid,bhnjd->bhnij', q, k) * decay
    q_dec = q * jnp.exp(cum)[..., None]
    k_dec = k * jnp.exp(cum[..., -1:] - cum)[..., None]
    last = jnp.exp(cum[..., -1])

    def step(state, xs):
        u_c, w_c, q_c, k_c, attn_c, last_c = xs
        v_new = u_c - jnp.einsum('bhck,bhkv->bhcv', w_c, state)
        o = jnp.einsum('bhck,bhkv->bhcv', q_c, state) + jnp.einsum('bhij,bhjv->bhiv', attn_c, v_new)
        state = state * last_c[..., None, None] + jnp.einsum('bhck,bhcv->bhkv', k_c, v_new)
        return state, o

    xs = tuple(jnp.moveaxis(t, 2, 0) for t in (u, w, q_dec, k_dec, attn, last))
    b, nh = q.shape[:2]
    state0 = jnp.zeros((b, nh, q.shape[-1], dv), jnp.float32)
    _, o = lax.scan(step, state0, xs)
    return from_chunks(jnp.moveaxis(o, 0, 2))

def gated_deltanet(h, w_in, w_conv, a_log, dt_bias, w_norm, w_out):
    b, t, _ = h.shape
    proj = h @ w_in
    qkv, z, beta_pre, a_pre = jnp.split(
        proj, [GDN_CONV_DIM, GDN_CONV_DIM + GDN_V_DIM, GDN_CONV_DIM + GDN_V_DIM + GDN_V_HEADS], axis=-1)
    qkv = causal_conv_silu(qkv, w_conv)
    q, k, v = jnp.split(qkv, [GDN_QK_DIM, 2 * GDN_QK_DIM], axis=-1)
    rep = GDN_V_HEADS // GDN_QK_HEADS
    q = l2_norm(q.reshape(b, t, GDN_QK_HEADS, GDN_HEAD_DIM)) * (GDN_HEAD_DIM ** -0.5)
    k = l2_norm(k.reshape(b, t, GDN_QK_HEADS, GDN_HEAD_DIM))
    q = jnp.repeat(q, rep, axis=2)
    k = jnp.repeat(k, rep, axis=2)
    v = v.reshape(b, t, GDN_V_HEADS, GDN_HEAD_DIM).astype(jnp.float32)
    beta = jax.nn.sigmoid(beta_pre.astype(jnp.float32))
    g = -jnp.exp(a_log.astype(jnp.float32)) * jax.nn.softplus(a_pre.astype(jnp.float32) + dt_bias.astype(jnp.float32))
    o = chunk_gated_delta_rule(q, k, v, g, beta)
    o = rms_norm(o, w_norm) * jax.nn.silu(z.reshape(b, t, GDN_V_HEADS, GDN_HEAD_DIM).astype(jnp.float32))
    return o.reshape(b, t, GDN_V_DIM).astype(h.dtype) @ w_out

def chunk_mlstm(q, k, v, i_pre, log_f):
    q, k, v = to_chunks(q), to_chunks(k), to_chunks(v)
    i_pre = to_chunks(i_pre, -jnp.inf)
    log_f = to_chunks(log_f)
    causal = jnp.tril(jnp.ones((CHUNK, CHUNK), dtype=bool))
    cum = jnp.cumsum(log_f, axis=-1)
    log_w = jnp.where(causal, cum[..., :, None] - cum[..., None, :] + i_pre[..., None, :], -jnp.inf)
    log_w_end = cum[..., -1:] - cum + i_pre
    qk = jnp.einsum('bhnid,bhnjd->bhnij', q, k)

    def step(carry, xs):
        c_mat, n_vec, m = carry
        q_c, k_c, v_c, cum_c, lw_c, lwe_c, qk_c = xs
        log_inter = cum_c + m[..., None]
        m_row = jnp.maximum(log_inter, jnp.max(lw_c, axis=-1))
        s_inter = jnp.exp(log_inter - m_row)
        w_intra = jnp.exp(lw_c - m_row[..., None]) * qk_c
        num = s_inter[..., None] * jnp.einsum('bhck,bhkv->bhcv', q_c, c_mat) \
            + jnp.einsum('bhij,bhjv->bhiv', w_intra, v_c)
        den = s_inter * jnp.einsum('bhck,bhk->bhc', q_c, n_vec) + jnp.sum(w_intra, axis=-1)
        h_c = num / jnp.maximum(jnp.abs(den), jnp.exp(-m_row))[..., None]
        log_keep = cum_c[..., -1] + m
        m_new = jnp.maximum(log_keep, jnp.max(lwe_c, axis=-1))
        s_keep = jnp.exp(log_keep - m_new)
        w_end = jnp.exp(lwe_c - m_new[..., None])
        c_mat = s_keep[..., None, None] * c_mat + jnp.einsum('bhc,bhck,bhcv->bhkv', w_end, k_c, v_c)
        n_vec = s_keep[..., None] * n_vec + jnp.einsum('bhc,bhck->bhk', w_end, k_c)
        return (c_mat, n_vec, m_new), h_c

    xs = tuple(jnp.moveaxis(t, 2, 0) for t in (q, k, v, cum, log_w, log_w_end, qk))
    b, nh, _, _, dk = q.shape
    dv = v.shape[-1]
    carry0 = (jnp.zeros((b, nh, dk, dv), jnp.float32), jnp.zeros((b, nh, dk), jnp.float32),
              jnp.zeros((b, nh), jnp.float32))
    _, hs = lax.scan(step, carry0, xs)
    return from_chunks(jnp.moveaxis(hs, 0, 2))

def mlstm(h, w_in, gate_bias, w_norm, w_out):
    b, t, _ = h.shape
    q, k, v, o, gates = jnp.split(
        h @ w_in, [MLSTM_QK_DIM, 2 * MLSTM_QK_DIM, 2 * MLSTM_QK_DIM + MLSTM_V_DIM,
                   2 * MLSTM_QK_DIM + 2 * MLSTM_V_DIM], axis=-1)
    q = q.reshape(b, t, MLSTM_HEADS, MLSTM_DQK).astype(jnp.float32)
    k = k.reshape(b, t, MLSTM_HEADS, MLSTM_DQK).astype(jnp.float32) * (MLSTM_DQK ** -0.5)
    v = v.reshape(b, t, MLSTM_HEADS, MLSTM_DV).astype(jnp.float32)
    gates = gates.astype(jnp.float32) + gate_bias.astype(jnp.float32)
    gates = GATE_SOFTCAP * jnp.tanh(gates / GATE_SOFTCAP)
    i_pre, f_pre = gates[..., :MLSTM_HEADS], gates[..., MLSTM_HEADS:]
    hs = chunk_mlstm(q, k, v, i_pre, jax.nn.log_sigmoid(f_pre))
    hs = rms_norm(hs, w_norm.reshape(MLSTM_HEADS, MLSTM_DV)) \
        * jax.nn.sigmoid(o.reshape(b, t, MLSTM_HEADS, MLSTM_DV).astype(jnp.float32))
    return hs.reshape(b, t, MLSTM_V_DIM).astype(h.dtype) @ w_out

def rope_tables(t):
    pos = jnp.arange(t, dtype=jnp.float32)
    inv_freq = ROPE_THETA ** (-jnp.arange(0, MLA_ROPE, 2, dtype=jnp.float32) / MLA_ROPE)
    ang = pos[:, None] * inv_freq[None, :]
    return jnp.cos(ang), jnp.sin(ang)

def apply_rope(x, cos, sin):
    x_pass, x_rot = x[..., :MLA_NOPE], x[..., MLA_NOPE:]
    x1, x2 = x_rot[..., :MLA_ROPE // 2], x_rot[..., MLA_ROPE // 2:]
    c = cos[None, :, None, :].astype(x.dtype)
    s = sin[None, :, None, :].astype(x.dtype)
    return jnp.concatenate([x_pass, x1 * c - x2 * s, x2 * c + x1 * s], axis=-1)

def causal_block_attention(q, k, v):
    b, t, nh, dq = q.shape
    dv = v.shape[-1]
    n_blk = -(-t // Q_BLOCK)
    qp = jnp.pad(q, ((0, 0), (0, n_blk * Q_BLOCK - t), (0, 0), (0, 0)))
    scale = dq ** -0.5
    k_pos = jnp.arange(t)

    def one_block(i):
        start = i * Q_BLOCK
        qb = lax.dynamic_slice_in_dim(qp, start, Q_BLOCK, axis=1)
        s = jnp.einsum('bqhd,bkhd->bhqk', qb, k).astype(jnp.float32) * scale
        q_pos = start + jnp.arange(Q_BLOCK)
        s = jnp.where(k_pos[None, :] <= q_pos[:, None], s, -jnp.inf)
        p = jax.nn.softmax(s, axis=-1).astype(v.dtype)
        return jnp.einsum('bhqk,bkhd->bqhd', p, v)

    o = lax.map(one_block, jnp.arange(n_blk))
    return jnp.moveaxis(o, 0, 1).reshape(b, n_blk * Q_BLOCK, nh, dv)[:, :t]

def mla(h, w_in, q_norm, w_uq, kv_norm, w_ukv, q_head_norm, k_head_norm, w_out):
    b, t, _ = h.shape
    c_q, c_kv, k_rope = jnp.split(h @ w_in, [MLA_Q_RANK, MLA_Q_RANK + MLA_KV_RANK], axis=-1)
    q = (rms_norm(c_q, q_norm) @ w_uq).reshape(b, t, MLA_HEADS, MLA_QK)
    kv = (rms_norm(c_kv, kv_norm) @ w_ukv).reshape(b, t, MLA_HEADS, MLA_NOPE + MLA_V)
    k_nope, v = kv[..., :MLA_NOPE], kv[..., MLA_NOPE:]
    k_rope = jnp.broadcast_to(k_rope[:, :, None, :], (b, t, MLA_HEADS, MLA_ROPE))
    k = jnp.concatenate([k_nope, k_rope], axis=-1)
    cos, sin = rope_tables(t)
    q = apply_rope(rms_norm(q, q_head_norm), cos, sin)
    k = apply_rope(rms_norm(k, k_head_norm), cos, sin)
    o = causal_block_attention(q, k, v)
    return o.reshape(b, t, MLA_HEADS * MLA_V) @ w_out

def squared_relu_mlp(h, w_up, w_down):
    a = jax.nn.relu(h @ w_up)
    return (a * a) @ w_down

def second_inputs(seed: int = 0) -> dict:
    key = jax.random.key(seed)
    keys = iter(jax.random.split(key, 40))
    f32 = jnp.float32

    def dense(shape, fan_in):
        return jax.random.normal(next(keys), shape, f32) * (fan_in ** -0.5)

    def gain(shape):
        return 1.0 + 0.02 * jax.random.normal(next(keys), shape, f32)

    x = jax.random.normal(next(keys), (BATCH, SEQ, D_MODEL), f32)
    meta_tokens = jax.random.normal(next(keys), (N_META, D_MODEL), f32)
    attn_norm = gain((DEPTH_2, D_MODEL))
    ffn_norm = gain((DEPTH_2, D_MODEL))
    ff_up = dense((DEPTH_2, D_MODEL, D_FF), D_MODEL)
    ff_down = dense((DEPTH_2, D_FF, D_MODEL), D_FF)
    gdn_in = dense((N_GDN_LAYERS, D_MODEL, GDN_IN), D_MODEL)
    gdn_conv = dense((N_GDN_LAYERS, GDN_CONV, GDN_CONV_DIM), GDN_CONV)
    gdn_a_log = jnp.log(jax.random.uniform(next(keys), (N_GDN_LAYERS, GDN_V_HEADS), f32, 1.0, 16.0))
    dt = jnp.exp(jax.random.uniform(next(keys), (N_GDN_LAYERS, GDN_V_HEADS), f32,
                                    np.float32(np.log(1e-3)), np.float32(np.log(1e-1))))
    gdn_dt_bias = dt + jnp.log(-jnp.expm1(-dt))
    gdn_norm = gain((N_GDN_LAYERS, GDN_HEAD_DIM))
    gdn_out = dense((N_GDN_LAYERS, GDN_V_DIM, D_MODEL), GDN_V_DIM)
    mlstm_in = dense((N_MLSTM_LAYERS, D_MODEL, MLSTM_IN), D_MODEL)
    ig_bias = 0.1 * jax.random.normal(next(keys), (N_MLSTM_LAYERS, MLSTM_HEADS), f32)
    fg_bias = jnp.linspace(3.0, 6.0, MLSTM_HEADS, dtype=f32)[None, :] \
        + 0.1 * jax.random.normal(next(keys), (N_MLSTM_LAYERS, MLSTM_HEADS), f32)
    mlstm_gate_bias = jnp.concatenate([ig_bias, fg_bias], axis=-1)
    mlstm_norm = gain((N_MLSTM_LAYERS, MLSTM_V_DIM))
    mlstm_out = dense((N_MLSTM_LAYERS, MLSTM_V_DIM, D_MODEL), MLSTM_V_DIM)
    mla_in = dense((N_MLA_LAYERS, D_MODEL, MLA_IN), D_MODEL)
    mla_q_norm = gain((N_MLA_LAYERS, MLA_Q_RANK))
    mla_uq = dense((N_MLA_LAYERS, MLA_Q_RANK, MLA_HEADS * MLA_QK), MLA_Q_RANK)
    mla_kv_norm = gain((N_MLA_LAYERS, MLA_KV_RANK))
    mla_ukv = dense((N_MLA_LAYERS, MLA_KV_RANK, MLA_HEADS * (MLA_NOPE + MLA_V)), MLA_KV_RANK)
    mla_q_head_norm = gain((N_MLA_LAYERS, MLA_QK))
    mla_k_head_norm = gain((N_MLA_LAYERS, MLA_QK))
    mla_out = dense((N_MLA_LAYERS, MLA_HEADS * MLA_V, D_MODEL), MLA_HEADS * MLA_V)
    return {'x': x, 'meta_tokens': meta_tokens, 'attn_norm': attn_norm, 'ffn_norm': ffn_norm,
            'ff_up': ff_up, 'ff_down': ff_down,
            'gdn_in': gdn_in, 'gdn_conv': gdn_conv, 'gdn_a_log': gdn_a_log, 'gdn_dt_bias': gdn_dt_bias,
            'gdn_norm': gdn_norm, 'gdn_out': gdn_out,
            'mlstm_in': mlstm_in, 'mlstm_gate_bias': mlstm_gate_bias, 'mlstm_norm': mlstm_norm,
            'mlstm_out': mlstm_out,
            'mla_in': mla_in, 'mla_q_norm': mla_q_norm, 'mla_uq': mla_uq, 'mla_kv_norm': mla_kv_norm,
            'mla_ukv': mla_ukv, 'mla_q_head_norm': mla_q_head_norm, 'mla_k_head_norm': mla_k_head_norm,
            'mla_out': mla_out}

def second_block(x, meta_tokens, attn_norm, ffn_norm, ff_up, ff_down,
              gdn_in, gdn_conv, gdn_a_log, gdn_dt_bias, gdn_norm, gdn_out,
              mlstm_in, mlstm_gate_bias, mlstm_norm, mlstm_out,
              mla_in, mla_q_norm, mla_uq, mla_kv_norm, mla_ukv, mla_q_head_norm, mla_k_head_norm,
              mla_out):
    b = x.shape[0]
    meta = jnp.broadcast_to(meta_tokens[None].astype(x.dtype), (b, N_META, x.shape[-1]))
    h = jnp.concatenate([meta, x], axis=1)
    for layer in range(DEPTH_2):
        kind, j = layer % N_MIXERS, layer // N_MIXERS
        hn = rms_norm(h, attn_norm[layer])
        if kind == 0:
            mix = gated_deltanet(hn, gdn_in[j], gdn_conv[j], gdn_a_log[j], gdn_dt_bias[j],
                                 gdn_norm[j], gdn_out[j])
        elif kind == 1:
            mix = mlstm(hn, mlstm_in[j], mlstm_gate_bias[j], mlstm_norm[j], mlstm_out[j])
        else:
            mix = mla(hn, mla_in[j], mla_q_norm[j], mla_uq[j], mla_kv_norm[j], mla_ukv[j],
                      mla_q_head_norm[j], mla_k_head_norm[j], mla_out[j])
        h = h + mix
        h = h + squared_relu_mlp(rms_norm(h, ffn_norm[layer]), ff_up[layer], ff_down[layer])
    return h[:, N_META:]


def setup_inputs(seed=0):
    out = dict(first_inputs(seed))
    for name, value in second_inputs(seed + 1).items():
        if name != "x":
            out[name + "_2"] = value
    return out


def reference(
    x, norm1_w, w_in, b_gate, diff_lq1, diff_lk1, diff_lq2, diff_lk2, diff_subln_w,
    chunk_rel_bias, w_branch_diff, w_branch_chunk, w_out, norm2_w, peer_wq, peer_keys, peer_u,
    peer_v, final_norm_w, meta_tokens_2, attn_norm_2, ffn_norm_2, ff_up_2, ff_down_2, gdn_in_2,
    gdn_conv_2, gdn_a_log_2, gdn_dt_bias_2, gdn_norm_2, gdn_out_2, mlstm_in_2,
    mlstm_gate_bias_2, mlstm_norm_2, mlstm_out_2, mla_in_2, mla_q_norm_2, mla_uq_2,
    mla_kv_norm_2, mla_ukv_2, mla_q_head_norm_2, mla_k_head_norm_2, mla_out_2,
):
    x = first_block(
        x, norm1_w, w_in, b_gate, diff_lq1, diff_lk1, diff_lq2, diff_lk2, diff_subln_w,
        chunk_rel_bias, w_branch_diff, w_branch_chunk, w_out, norm2_w, peer_wq, peer_keys,
        peer_u, peer_v, final_norm_w,
    )
    return second_block(
        x, meta_tokens_2, attn_norm_2, ffn_norm_2, ff_up_2, ff_down_2, gdn_in_2, gdn_conv_2,
        gdn_a_log_2, gdn_dt_bias_2, gdn_norm_2, gdn_out_2, mlstm_in_2, mlstm_gate_bias_2,
        mlstm_norm_2, mlstm_out_2, mla_in_2, mla_q_norm_2, mla_uq_2, mla_kv_norm_2, mla_ukv_2,
        mla_q_head_norm_2, mla_k_head_norm_2, mla_out_2,
    )


_drawn_inputs = setup_inputs


def setup_inputs(seed=0):
    import zlib

    import numpy as np

    out = dict(_drawn_inputs(seed))
    spreads = {}
    factors = {'b_gate': 8.0,
     'diff_lk1': 2.774,
     'diff_lq2': 2.903,
     'diff_subln_w': 4.244,
     'chunk_rel_bias': 6.502,
     'norm2_w': 8.0,
     'peer_u': 2.943,
     'gdn_norm_2': 4.399,
     'mlstm_norm_2': 27.931,
     'ffn_norm_2': 3.299}
    for name, (base, spread) in spreads.items():
        noise = np.random.default_rng([zlib.crc32(name.encode()), seed]).standard_normal(out[name].shape)
        drawn = base * np.exp(spread * noise) if base else spread * noise
        out[name] = jnp.asarray(drawn.astype(out[name].dtype))
    for name, factor in factors.items():
        out[name] = (out[name] * factor).astype(out[name].dtype)
    return out
```

```python
from contextlib import ExitStack

import numpy as np
import concourse.bass as bass
from concourse import mybir

ALU = mybir.AluOpType
ACT = mybir.ActivationFunctionType
F32 = mybir.dt.float32
U32 = mybir.dt.uint32
AX = mybir.AxisListType.X

NEG = -1.0e30
NSLOT = 11
HALVES = [(0, 272), (272, 528)]
DBG = []


class Engine:

    def __init__(self, sem):
        self.sem, self.n, self.items = sem, 0, []

    def do(self, fn, *after):
        self.n += 1
        self.items.append((flat(after), fn, self.sem, 1))
        return (self.sem, self.n)

    def silent(self, fn, *after):
        self.items.append((flat(after), fn, None, 0))

    def dma(self, fn, line, *after):
        line.n += 16
        self.items.append((flat(after), fn, line.sem, 16))
        return (line.sem, line.n)

    def now(self):
        return (self.sem, self.n)

    def play(self, eng):
        seen = {}
        for after, fn, sem, amount in self.items:
            best = {}
            for s, v in after:
                best[s] = max(best.get(s, 0), v)
            for s, v in best.items():
                if v > seen.get(s, 0):
                    eng.wait_ge(s, v)
                    seen[s] = v
            if fn is None:
                continue
            ins = fn(eng)
            if sem is not None:
                ins.then_inc(sem, amount)


class Line:

    def __init__(self, sem):
        self.sem, self.n = sem, 0


class Ring:

    def __init__(self, bufs):
        self.bufs, self.free = bufs, [(j, []) for j in range(len(bufs))]

    def take(self):
        assert self.free, "no buffer has been given back"
        j, toks = self.free.pop(0)
        return self.bufs[j], toks, j

    def give(self, j, *toks):
        self.free.append((j, flat(toks)))


def flat(x):
    if x is None:
        return []
    if isinstance(x, list) or (isinstance(x, tuple) and not (len(x) == 2 and isinstance(x[1], int))):
        return [t for y in x for t in flat(y)]
    return [x]


def weave(main, side, ratio=1):
    m = s = True
    while m or s:
        if m:
            m = next(main, None) is not None
        for _ in range(ratio):
            if s:
                s = next(side, None) is not None


def none():
    return iter(())


def consts():
    c = {}
    p = np.arange(128)[:, None]
    f = np.arange(128)[None, :]
    c["ident"] = (p == f).astype(np.float32)
    blk = (p // 64) == (f // 64)
    j, i = p % 64, f % 64
    c["mask"] = np.where(blk & (i >= j), 0.0, NEG).astype(np.float32)
    for n, b in enumerate((1, 2, 4, 8, 16, 32)):
        m = blk & (i // (2 * b) == j // (2 * b)) & (i % (2 * b) >= b) & (j % (2 * b) < b)
        c[f"lev{n}"] = m.astype(np.float32)
    k = np.arange(512)[None, :]
    nd = -np.abs(p - (k - 384)).astype(np.float32)
    nd[0:64, 448:512] = NEG
    c["negdist"] = nd
    c["iota"] = np.broadcast_to(f, (128, 128)).astype(np.float32)
    c["reset"] = np.broadcast_to((np.arange(576) % 64 != 0), (128, 576)).astype(np.float32)
    return c


CONST_SMALL = ["ident", "mask", "lev0", "lev1", "lev2", "lev3", "lev4", "lev5", "iota"]
COLS = dict(norm1=(0, 8), norm2=(8, 8), final=(16, 8), attn0=(24, 8), attn1=(32, 8), ffn0=(40, 8), ffn1=(48, 8),
            bgate=(56, 16), conv=(72, 128), gdnn=(200, 1), mln=(201, 8), subln=(209, 1))


def build(nc, X, out, scratch, dbg):
    ctx = ExitStack()
    with ctx:
        def sem(name):
            return ctx.enter_context(nc.semaphore(name))

        NCOL = (212863 - NSLOT * 4096 - 256) // 4
        ring_t = ctx.enter_context(nc.sbuf_tensor("ring", [128, NSLOT * 1024], F32))
        arena = ctx.enter_context(nc.sbuf_tensor("arena", [128, NCOL], F32))
        banks = [ctx.enter_context(nc.psum_tensor(f"bank{i}", [128, 512], F32)) for i in range(8)]

        PE, DV, AC, PO, SP = (Engine(sem(n)) for n in ("s_pe", "s_dv", "s_ac", "s_po", "s_sp"))
        ENGS = (PE, DV, AC, PO)

        top = [0]

        def alloc(*dims):
            n = int(np.prod(dims))
            o = top[0]
            top[0] += n
            assert top[0] <= NCOL, (top[0], NCOL)
            a = arena[:, o:o + n]
            if len(dims) == 2:
                return a.rearrange("p (a b) -> p a b", a=dims[0])
            if len(dims) == 3:
                return a.rearrange("p (a b c) -> p a b c", a=dims[0], b=dims[1])
            return a

        def fence():
            toks = [e.now() for e in ENGS]
            for e in ENGS:
                e.items.append((toks, None, None, 0))
            return toks

        def act(out, in_, func, *after, bias=None, scale=1.0, accum=None):
            kw = dict(scale=scale)
            if bias is not None:
                kw["bias"] = bias
            if accum is not None:
                kw["accum_out"] = accum
            return AC.do(lambda e: e.activation(out, in_, func, **kw), *after)

        def copy(out, in_, *after):
            return AC.do(lambda e: e.activation(out, in_, ACT.Copy), *after)

        def tt(E, out, a, b, op, *after):
            return E.do(lambda e: e.tensor_tensor(out, a, b, op), *after)

        def ts(E, out, a, s1, s2, op0, op1, *after):
            if op1 is None:
                return E.do(lambda e: e.tensor_scalar(out, a, s1, None, op0), *after)
            return E.do(lambda e: e.tensor_scalar(out, a, s1, s2, op0, op1), *after)

        def stt(out, a, s, b, op0, op1, *after):
            return DV.do(lambda e: e.scalar_tensor_tensor(out=out, in0=a, scalar=s, in1=b, op0=op0, op1=op1), *after)

        def recip(out, in_, *after):
            return DV.do(lambda e: e.reciprocal(out, in_), *after)

        def tcopy(E, out, in_, *after):
            return E.do(lambda e: e.tensor_copy(out, in_), *after)

        def reduce(out, in_, op, *after):
            return DV.do(lambda e: e.tensor_reduce(out=out, in_=in_, op=op, axis=AX), *after)

        def dma(E, line, out, in_, *after):
            return E.dma(lambda e: e.dma_start(out, in_), line, *after)

        def mset(E, out, v, *after):
            return E.do(lambda e: e.memset(out, v), *after)

        def mm(out, terms, *after, start=True, stop=True):
            tok = None
            for i, (l, r) in enumerate(terms):
                s0, s1 = start and i == 0, stop and i == len(terms) - 1

                def fn(e, l=l, r=r, s0=s0, s1=s1):
                    return e.matmul(out, l, r, start=s0, stop=s1)
                if i == len(terms) - 1:
                    tok = PE.do(fn, *(after if i == 0 else ()))
                else:
                    PE.silent(fn, *(after if i == 0 else ()))
            return tok

        def tr(out, in_, *after):
            return PE.do(lambda e: e.transpose(out, in_, IDENT), *after)

        lines = [Line(sem(f"s_w{i}")) for i in range(NSLOT)]
        WR = Ring([ring_t[:, i * 1024:(i + 1) * 1024] for i in range(NSLOT)])

        def load(src):
            buf, free, j = WR.take()
            tok = dma(SP, lines[j], buf, src, free)
            return buf.rearrange("p (k f) -> p k f", f=128), tok, j

        l_c = Line(sem("s_c"))
        n_once = [0]

        def once():
            n_once[0] += 1
            return Line(sem(f"s_once{n_once[0]}"))

        CS = {}
        for n in CONST_SMALL:
            CS[n] = alloc(128)
        CB_ = alloc(210)
        ROWP = alloc(8)
        ct = []
        for i, n in enumerate(CONST_SMALL):
            ct.append(dma(AC, l_c, CS[n], X["cst"][:, i * 128:(i + 1) * 128]))
        ct.append(dma(AC, l_c, CB_, X["cols"][:, :]))
        ct.append(dma(AC, l_c, ROWP[0:16, 0:4], X["rows"][:, :]))
        C0 = ct[-1]
        IDENT = CS["ident"]
        ONES = alloc(128)
        ONE = ONES[:, 0:1]
        EPS = alloc(1)
        t = [mset(PO, ONES, 1.0), mset(PO, EPS, 1e-6)]
        K0 = [C0, t]
        for e in (PE, DV, AC, PO):
            e.items.append((flat(K0), None, None, 0))

        def col(name, i=0):
            return CB_[:, COLS[name][0] + i:COLS[name][0] + i + 1]

        PD = Ring([banks[i][:, :] for i in range(3)])
        PA = Ring([banks[i][:, :] for i in range(3, 8)])

        H = alloc(8, 528)
        XN = alloc(8, 528)
        SQ = Ring([alloc(512) for _ in range(2)])
        RT = Ring([alloc(528) for _ in range(2)])
        base = top[0]

        l_x = Line(sem("s_x"))
        tx = dma(AC, l_x, H[:, :, 16:528], X["x"].rearrange("p (k t) -> p k t", k=8))
        tm = dma(AC, l_x, H[:, :, 0:16], X["meta"].rearrange("p (k t) -> p k t", k=8))
        tx = [tx, tm]

        def dump(name, ap, *after):
            if name in dbg:
                t = dma(AC, l_dbg, dbg[name], ap, *after)
                for e in (PE, DV, AC, PO, SP):
                    e.items.append(([t], None, None, 0))

        l_dbg = Line(sem("s_dbg"))

        def inv_rms(parts, n, scale, R, lhs, *after, bias=True, ring=None):
            ring = ring or PD
            ps, pw, pj = ring.take()
            for i, a in enumerate(parts):
                sq, sw, sj = SQ.take()
                t1 = act(sq[:, 0:n], a, ACT.Square, sw, *after)
                t2 = mm(ps[:, 0:n], [(lhs, sq[:, 0:n])], t1, pw if i == 0 else None,
                        start=i == 0, stop=i == len(parts) - 1)
                SQ.give(sj, t2)
            t3 = act(R, ps[:, 0:n], ACT.Sqrt, t2, bias=EPS, scale=scale)
            ring.give(pj, t3)
            return recip(R, R, t3)

        def rmsnorm(wname, dst, halves, src_tok, free):
            toks = []
            for a, b in halves:
                r, rw, rj = RT.take()
                t = inv_rms([H[:, k, a:b] for k in range(8)], b - a, 1.0 / 1024, r[:, 0:b - a], ONES, src_tok, rw)
                for k in range(8):
                    t2 = stt(dst[:, k, a:b], H[:, k, a:b], col(wname, k), r[:, 0:b - a], ALU.mult, ALU.mult, t, free)
                    toks.append(t2)
                RT.give(rj, t2)
            return toks[-1]

        BIAS = alloc(8, 512)
        ND = alloc(512)
        tb = dma(AC, once(), ND, X["negdist"][:, :])
        tb2 = dma(AC, once(), BIAS, X["bias"].rearrange("p (k t) -> p k t", k=8))
        LQ = alloc(4, 64)
        tb3 = dma(AC, once(), LQ, X["lq"].rearrange("p (k t) -> p k t", k=4))
        t_b0 = mset(PO, BIAS[0:64, :, 448:512], NEG, tb3)
        LAM = alloc(8)
        LP = alloc(2, 64)
        t = tt(DV, LP[:, 0, :], LQ[:, 0, :], LQ[:, 1, :], ALU.mult, tb3)
        t = tt(DV, LP[:, 1, :], LQ[:, 2, :], LQ[:, 3, :], ALU.mult, tb3)
        t = reduce(LAM[:, 0:2], LP, ALU.add, t)
        t = act(LAM[:, 2:4], LAM[:, 0:2], ACT.Exp, t)
        t = tt(DV, LAM[:, 4:5], LAM[:, 2:3], LAM[:, 3:4], ALU.subtract, t)
        t_lam = ts(DV, LAM[:, 5:6], LAM[:, 4:5], 0.8 - 0.6, -1.0, ALU.add, ALU.mult, t)
        SUB = LAM[:, 6:7]
        t_sub = ts(DV, SUB, col("subln"), 1.0 - (0.8 - 0.6), None, ALU.mult, None, t_lam)

        t_xn = rmsnorm("norm1", XN, [(16, 528)], tx, None)

        OD = alloc(8, 512)
        OC = alloc(4, 512)
        QT = Ring([alloc(512) for _ in range(2)])
        KT = Ring([alloc(512) for _ in range(2)])
        VT = Ring([alloc(4, 128) for _ in range(2)])
        S1 = Ring([alloc(512) for _ in range(4)])
        AT = Ring([alloc(512) for _ in range(2)])
        SC = Ring([alloc(8) for _ in range(4)])
        OO = Ring([alloc(512) for _ in range(2)])
        attn_out = {}
        unit = {}

        def xk(k):
            return XN[:, k, 16:528]

        def proj(u):
            st = {}
            for kind in range(3):
                w, wt, wj = load(X["w_att"][3 * u + kind])
                ps, pw, pj = PD.take()
                if kind < 2:
                    r = (QT, KT)[kind]
                    b, bw, bj = r.take()
                    tp = mm(ps, [(w[:, k, :], xk(k)) for k in range(8)], wt, pw, t_xn)
                    te = copy(b, ps, tp, bw)
                    st["qk"[kind]] = (b, te, bj)
                    yield 1
                else:
                    b, bw, bj = VT.take()
                    for tl in range(4):
                        tp = mm(ps[:, tl * 128:(tl + 1) * 128],
                                [(XN[:, k, 16 + tl * 128:144 + tl * 128], w[:, k, :]) for k in range(8)],
                                wt, pw, t_xn)
                        if tl == 1:
                            yield 1
                    te = copy(b, ps.rearrange("p (a b) -> p a b", a=4), tp, bw)
                    st["v"] = (b, te, bj)
                WR.give(wj, tp)
                PD.give(pj, te)
            unit[u] = st
            yield 1

        def attend(u):
            st = unit[u]
            (q, qt, qj), (k, kt, kj), (v, vt, vj) = st["q"], st["k"], st["v"]
            diff = u < 8
            po, pow_, poj = PA.take()
            t_last = None
            for i in range(4):
                N = 128 * (i + 1)
                probs = []
                for m in range(2):
                    lo = m * 64
                    ps, pw, pj = PA.take()
                    tp = mm(ps[:, 0:N], [(q[lo:lo + 64, i * 128:(i + 1) * 128], k[lo:lo + 64, 0:N])],
                            qt, kt, pw)
                    s, sw, sj = S1.take()
                    c, cw, cj = SC.take()
                    if diff:
                        slope = 2.0 ** (-(u + 1))
                        t1 = stt(s[:, 0:N], ND[:, 512 - N:512], slope * 8.0, ps[:, 0:N], ALU.mult, ALU.add,
                                 tp, sw, tb)
                        sc = 0.125
                    else:
                        t1 = stt(s[:, 0:N], ps[:, 0:N], 0.125, BIAS[:, 2 * (u - 8) + m, 512 - N:512],
                                 ALU.mult, ALU.add, tp, sw, t_b0)
                        sc = 1.0
                    PA.give(pj, t1)
                    t2 = reduce(c[:, 0:1], s[:, 0:N], ALU.max, t1, cw)
                    t3 = ts(DV, c[:, 1:2], c[:, 0:1], -sc, None, ALU.mult, None, t2)
                    t4 = act(s[:, 0:N], s[:, 0:N], ACT.Exp, t3, bias=c[:, 1:2], scale=sc, accum=c[:, 2:3])
                    t5 = recip(c[:, 3:4], c[:, 2:3], t4)
                    probs.append((s, sj, c, cj, t5))
                yield 1
                (s1, j1, c1, d1, t1), (s2, j2, c2, d2, t2) = probs
                if diff:
                    t = tt(DV, c2[:, 4:5], c2[:, 3:4], LAM[:, 5:6], ALU.mult, t2, t_lam)
                    t = ts(DV, s2[:, 0:N], s2[:, 0:N], c2[:, 4:5], None, ALU.mult, None, t)
                    t = stt(s1[:, 0:N], s1[:, 0:N], c1[:, 3:4], s2[:, 0:N], ALU.mult, ALU.add, t, t1)
                    S1.give(j2, t)
                    SC.give(d1, t)
                    SC.give(d2, t)
                    srcs = [(s1, j1, t, 0)]
                else:
                    ta = ts(DV, s1[:, 0:N], s1[:, 0:N], c1[:, 3:4], None, ALU.mult, None, t1)
                    tb_ = ts(DV, s2[:, 0:N], s2[:, 0:N], c2[:, 3:4], None, ALU.mult, None, t2)
                    SC.give(d1, ta)
                    SC.give(d2, tb_)
                    srcs = [(s1, j1, ta, 0), (s2, j2, tb_, 1)]
                for s, sj, t, m in srcs:
                    ps, pw, pj = PA.take()
                    for kt_ in range(i + 1):
                        tp = tr(ps[:, kt_ * 128:(kt_ + 1) * 128], s[:, kt_ * 128:(kt_ + 1) * 128], t, pw)
                    S1.give(sj, tp)
                    a, aw, aj = AT.take()
                    te = copy(a[:, 0:N], ps[:, 0:N], tp, aw)
                    PA.give(pj, te)
                    yield 1
                    if diff:
                        o, vs = po[:, i * 128:(i + 1) * 128], lambda n: v[:, n, :]
                    else:
                        o = po[m * 64:m * 64 + 64, i * 128:(i + 1) * 128]
                        vs = lambda n, m=m: v[:, n, m * 64:m * 64 + 64]
                    t_last = mm(o, [(vs(n), a[:, n * 128:(n + 1) * 128]) for n in range(i + 1)], te, vt, pow_)
                    AT.give(aj, t_last)
                    yield 1
            QT.give(qj, t_last)
            KT.give(kj, t_last)
            VT.give(vj, t_last)
            if diff:
                o, ow, oj = OO.take()
                t1 = copy(o, po, t_last, ow)
                PA.give(poj, t1)
                r, rw, rj = RT.take()
                t2 = inv_rms([o], 512, 1.0 / 128, r[:, 0:512], ONES, t1, rw, ring=PA)
                t3 = stt(OD[:, u, :], o, SUB, r[:, 0:512], ALU.mult, ALU.mult, t2, t_sub)
                RT.give(rj, t3)
                OO.give(oj, t3)
                attn_out[u] = t3
            else:
                t1 = copy(OC[:, u - 8, :], po, t_last)
                PA.give(poj, t1)
                attn_out[u] = t1
            yield 1

        for u in range(13):
            weave(proj(u) if u < 12 else none(), attend(u - 1) if u else none(), 4)

        MG = alloc(8, 512)
        G1 = Ring([alloc(512) for _ in range(4)])
        t_d, t_c = attn_out[7], attn_out[11]
        wc = None
        t_mg = []
        for fb in range(8):
            gs = []
            for n in range(2):
                w, wt, wj = load(X["w_gate"][2 * fb + n])
                ps, pw, pj = PD.take()
                tp = mm(ps, [(w[:, k, :], xk(k)) for k in range(8)], wt, pw)
                WR.give(wj, tp)
                g, gw, gj = G1.take()
                t1 = act(g, ps, ACT.Sigmoid, tp, gw, bias=col("bgate", 8 * n + fb))
                PD.give(pj, t1)
                gs.append((g, gj, t1))
            w, wt, wj = load(X["w_bd"][fb])
            ps, pw, pj = PD.take()
            tp = mm(ps, [(w[:, k, :], OD[:, k, :]) for k in range(8)], wt, pw, t_d)
            WR.give(wj, tp)
            g, gj, tg = gs[0]
            ta = tt(DV, g, g, ps, ALU.mult, tp, tg)
            PD.give(pj, ta)
            if fb % 2 == 0:
                wc = load(X["w_bc"][fb // 2])
            ps, pw, pj = PD.take()
            tp = mm(ps, [(wc[0][:, 4 * (fb % 2) + k, :], OC[:, k, :]) for k in range(4)], wc[1], pw, t_c)
            if fb % 2:
                WR.give(wc[2], tp)
            g2, gj2, tg2 = gs[1]
            tb_ = tt(DV, g2, g2, ps, ALU.mult, tp, tg2)
            PD.give(pj, tb_)
            t = tt(DV, MG[:, fb, :], g, g2, ALU.add, tb_, ta)
            t_mg.append(t)
            G1.give(gj, t)
            G1.give(gj2, t)
        t_h = None
        for fb in range(8):
            w, wt, wj = load(X["w_out"][fb])
            ps, pw, pj = PD.take()
            tp = mm(ps, [(w[:, k, :], MG[:, k, :]) for k in range(8)], wt, pw, t_mg[-1])
            WR.give(wj, tp)
            t_h = tt(DV, H[:, fb, 16:528], H[:, fb, 16:528], ps, ALU.add, tp)
            PD.give(pj, t_h)
        dump("h1", H, t_h)

        fence()
        top[0] = base
        t_xn = rmsnorm("norm2", XN, [(16, 528)], t_h, PE.now())
        TT_ = alloc(3, 512)
        after_tt = top[0]
        KEY = alloc(8, 128)
        tk = dma(AC, once(), KEY, X["keys"].rearrange("p (k t) -> p k t", k=8),
                 DV.now(), PE.now(), PO.now())
        QP = alloc(8, 512)
        t_q = None
        for h in range(8):
            w, wt, wj = load(X["w_q"][h])
            ps, pw, pj = PD.take()
            tp = mm(ps, [(w[:, k, :], xk(k)) for k in range(8)], wt, pw, t_xn)
            WR.give(wj, tp)
            t_q = copy(QP[:, h, :], ps, tp)
            PD.give(pj, t_q)
        SS = Ring([alloc(16, 128)])
        S2 = Ring([alloc(256) for _ in range(2)])
        VV = alloc(2, 8, 16)
        II = alloc(2, 8, 16)
        IF = alloc(2, 8, 16)
        CA = alloc(8, 256)
        CV = alloc(8, 16)
        CI = alloc(8, 16)
        AB = alloc(2, 128)
        ABF = alloc(2, 128)
        EQ = alloc(128, 16)
        TK = alloc(3, 128)
        RS = alloc(16)
        iota16 = CS["iota"][:, 0:16]
        t_sel = {}
        for tl in range(4):
            ss, sw, sj = SS.take()
            for s in range(2):
                for hh in range(2):
                    ps, pw, pj = PA.take()
                    for h in range(4):
                        tp = mm(ps[:, h * 128:(h + 1) * 128],
                                [(QP[s * 64:s * 64 + 64, 4 * hh + h, tl * 128:(tl + 1) * 128],
                                  KEY[s * 64:s * 64 + 64, 4 * hh + h, :])], t_q, tk, pw)
                    a0 = s * 8 + hh * 4
                    te = copy(ss[:, a0:a0 + 4, :], ps.rearrange("p (a b) -> p a b", a=4), tp, sw)
                    PA.give(pj, te)

            def top16(src, n, vals, idxs, t):
                s2, s2w, s2j = S2.take()
                a = DV.do(lambda e: e.max(vals[:, 0:8], src), t)
                b = DV.do(lambda e: e.max_index(idxs[:, 0:8].bitcast(U32), vals[:, 0:8], src), a)
                b = DV.do(lambda e: e.match_replace(out=s2[:, 0:n], in_to_replace=vals[:, 0:8], in_values=src,
                                                    imm_value=-3.0e38), a, s2w)
                c = DV.do(lambda e: e.max(vals[:, 8:16], s2[:, 0:n]), b)
                d = DV.do(lambda e: e.max_index(idxs[:, 8:16].bitcast(U32), vals[:, 8:16], s2[:, 0:n]), c)
                S2.give(s2j, d)
                return d

            for s in range(2):
                for h in range(8):
                    t = top16(ss[:, s * 8 + h, :], 128, VV[:, s, h, :], II[:, s, h, :], te)
            SS.give(sj, t)
            t1 = tcopy(DV, IF, II.bitcast(U32), t)
            t = tt(DV, CA.rearrange("p h (a b) -> p h a b", a=16),
                   VV[:, 0, :, :].unsqueeze(3).to_broadcast([128, 8, 16, 16]),
                   VV[:, 1, :, :].unsqueeze(2).to_broadcast([128, 8, 16, 16]), ALU.add, t1)
            for h in range(8):
                t = top16(CA[:, h, :], 256, CV[:, h, :], CI[:, h, :], t)
            CIu = CI.rearrange("p a b -> p (a b)").bitcast(U32)
            t1 = ts(DV, AB[:, 0, :].bitcast(U32), CIu, 4, None, ALU.logical_shift_right, None, t)
            t2 = ts(DV, AB[:, 1, :].bitcast(U32), CIu, 15, None, ALU.bitwise_and, None, t)
            t3 = tcopy(DV, ABF, AB.bitcast(U32), t1, t2)
            for s in range(2):
                t4 = tt(DV, EQ, ABF[:, s, :].unsqueeze(2).to_broadcast([128, 128, 16]),
                        iota16.unsqueeze(1).to_broadcast([128, 128, 16]), ALU.is_equal, t3)
                e4 = EQ.rearrange("p (h k) a -> p h k a", h=8)
                t4 = tt(DV, e4, e4, IF[:, s, :, :].unsqueeze(2).to_broadcast([128, 8, 16, 16]), ALU.mult, t4)
                t3 = reduce(TK[:, s, :], EQ, ALU.add, t4, t_sel.get(tl - 1))
            G3 = TK[:, 2, :].rearrange("p (h k) -> p h k", h=8)
            MX = RS[:, 8:16]
            t4 = tcopy(DV, MX, CV[:, :, 0:1].rearrange("p a b -> p (a b)"), t3)
            t4 = tt(DV, CV, CV, MX.unsqueeze(2).to_broadcast([128, 8, 16]), ALU.subtract, t4)
            t5 = act(G3, CV, ACT.Exp, t4)
            t5 = reduce(RS[:, 0:8], G3, ALU.add, t5)
            t5 = recip(RS[:, 0:8], RS[:, 0:8], t5)
            t5 = tt(DV, G3, G3, RS[:, 0:8].unsqueeze(2).to_broadcast([128, 8, 16]), ALU.mult, t5)
            ps, pw, pj = PA.take()
            for n in range(3):
                tp = tr(ps[:, n * 128:(n + 1) * 128], TK[:, n, :], t5, pw)
            te = copy(TT_[:, :, tl * 128:(tl + 1) * 128], ps[:, 0:384].rearrange("p (a b) -> p a b", a=3), tp)
            PA.give(pj, te)
            t_sel[tl] = tp
            t_selc = te
        dump("tt", TT_, t_selc)
        fence()
        top[0] = after_tt
        OH1 = Ring([alloc(8, 128) for _ in range(2)])
        OH2 = Ring([alloc(8, 128) for _ in range(2)])
        GB = Ring([alloc(128, 64) for _ in range(2)])
        l_g = [Line(sem("s_g0")), Line(sem("s_g1"))]
        iota = CS["iota"]
        t_g = []
        for tb_i in range(8):
            gb, gbw, gbj = GB.take()
            for q8 in range(8):
                t0 = tb_i * 64 + q8 * 8
                o1, w1, j1 = OH1.take()
                o2, w2, j2 = OH2.take()
                ta = tt(DV, o1, iota.unsqueeze(1).to_broadcast([128, 8, 128]),
                        TT_[:, 0, t0:t0 + 8].unsqueeze(2).to_broadcast([128, 8, 128]), ALU.is_equal, t_selc, w1)
                for n in range(8):
                    tb_ = ts(DV, o2[:, n, :], iota, TT_[:, 1, t0 + n:t0 + n + 1], TT_[:, 2, t0 + n:t0 + n + 1],
                             ALU.is_equal, ALU.mult, t_selc, w2)
                for q in range(2):
                    ps, pw, pj = PA.take()
                    for n in range(4):
                        tp = mm(ps[:, n * 128:(n + 1) * 128], [(o1[:, 4 * q + n, :], o2[:, 4 * q + n, :])],
                                ta, tb_, pw)
                    c0 = q8 * 8 + q * 4
                    te = copy(gb[:, :, c0:c0 + 4].rearrange("p b t -> p t b"),
                              ps.rearrange("p (t b) -> p t b", t=4), tp, gbw)
                    PA.give(pj, te)
                OH1.give(j1, tp)
                OH2.give(j2, tp)
            td = dma(PO, l_g[gbj], scratch[tb_i], gb, te)
            GB.give(gbj, td)
            t_g.append(td)

        fz = fence()
        top[0] = base
        GJ = Ring([alloc(8, 8, 64) for _ in range(2)])
        AA = Ring([alloc(8, 512) for _ in range(2)])
        l_j = [Line(sem("s_j0")), Line(sem("s_j1"))]
        pend = None

        def down(job):
            a, aj, ta, ws = job
            for db in range(8):
                ps, pw, pj = PA.take()
                tp = mm(ps, [(ws[j][0][:, db, :], a[:, j, :]) for j in range(8)], [x[1] for x in ws], ta, pw)
                th = tt(DV, H[:, db, 16:528], H[:, db, 16:528], ps, ALU.add, tp)
                PA.give(pj, th)
            for x in ws:
                WR.give(x[2], tp)
            AA.give(aj, tp)
            return th

        for jg in range(16):
            gj, gw, gjj = GJ.take()
            tg = dma(SP, l_j[gjj], gj.rearrange("p b j t -> p b (j t)"),
                     scratch[:, :, jg * 8:(jg + 1) * 8, :].rearrange("b p j t -> p b (j t)"), t_g, gw, fz)
            a, aw, aj = AA.take()
            for j in range(8):
                w, wt, wj = load(X["u"][jg * 8 + j])
                ps, pw, pj = PD.take()
                tp = mm(ps, [(w[:, k, :], xk(k)) for k in range(8)], wt, pw)
                WR.give(wj, tp)
                t1 = act(a[:, j, :], ps, ACT.Gelu, tp, aw)
                PD.give(pj, t1)
                av = a[:, j, :].rearrange("p (b t) -> p b t", b=8)
                ta = tt(DV, av, av, gj[:, :, j, :], ALU.mult, t1, tg)
            GJ.give(gjj, ta)
            if pend is not None:
                t_h = down(pend)
            pend = (a, aj, ta, [load(X["v"][jg * 8 + j]) for j in range(8)]) if False else (a, aj, ta, None)
            ws = [load(X["v"][jg * 8 + j]) for j in range(8)]
            t_h = down((a, aj, ta, ws))
            pend = None
        dump("h2", H, t_h)

        fence()
        top[0] = base
        t_h = rmsnorm("final", H, [(16, 528)], t_h, None)
        dump("h3", H, t_h)

        def hn(k, a, b):
            return XN[:, k, a:b]

        def expand(row, dst, nh, t):
            for d in range(2):
                t = tcopy(PO, dst[0:nh, :, d, :], row, t)
            return t

        def to_cols(src, nh, dst, t, full=None):
            ps, pw, pj = PA.take()
            for c in range(9):
                tp = mm(ps[:, c * nh:(c + 1) * nh], [(src[0:nh, c, :], IDENT[0:nh, 0:nh])], t, pw)
            v = ps[:, 0:9 * nh].rearrange("p (c h e) -> p c h e", c=9, e=2)
            r = []
            if dst is not None:
                for d in range(2):
                    lo = d * 64
                    r.append(copy(dst[lo:lo + 64, :, :], v[lo:lo + 64, :, :, d], tp))
            if full is not None:
                r.append(copy(full, ps[:, 0:9 * nh].rearrange("p (c h) -> p c h", c=9), tp))
            PA.give(pj, r)
            return r

        def row_bcast(row, h0, g, ps, *after):
            v = ps[:, 0:384].rearrange("p (c h i) -> p c h i", c=3, h=2)
            nh = row.shape[0]
            for d in range(2):
                tp = mm(v[:, :, d, :], [(IDENT[0:nh, h0 + d:h0 + d + 1].to_broadcast([nh, 128]), row[:, 3 * g:3 * g + 3, :])], *after)
            return tp

        def log_part(dst, y, tmp, nh, t, sign):
            t1 = act(tmp, y, ACT.Abs, t)
            t1 = act(tmp, tmp, ACT.Exp, t1, scale=-1.0)
            t1 = act(tmp, tmp, ACT.Ln, t1, bias=ONES[0:nh, 0:1])
            t2 = ts(DV, dst, y, sign, 0.0, ALU.mult, ALU.max, t)
            return tt(DV, dst, dst, tmp, ALU.add, t1, t2)

        def chunks(h0, c0):
            return [(0, 16, slice(0, 1), slice(48, 64)), (16, 272, slice(1, 5), slice(0, 64))] if c0 == 0 else \
                [(0, 256, slice(5, 9), slice(0, 64))]

        def ffn(layer):
            nonlocal t_h
            fence()
            top[0] = base
            t_x = rmsnorm(f"ffn{layer}", XN, HALVES, t_h, PE.now())
            FF = alloc(32, 528)
            ta = None
            for fb in range(32):
                w, wt, wj = load(X[f"up{layer}"][fb])
                for a, b in HALVES:
                    ps, pw, pj = PD.take()
                    tp = mm(ps[:, 0:b - a], [(w[:, k, :], hn(k, a, b)) for k in range(8)], wt, pw, t_x)
                    t1 = act(FF[:, fb, a:b], ps[:, 0:b - a], ACT.Relu, tp)
                    PD.give(pj, t1)
                    ta = tt(DV, FF[:, fb, a:b], FF[:, fb, a:b], FF[:, fb, a:b], ALU.mult, t1)
                WR.give(wj, tp)
            for fb in range(8):
                ws = [load(X[f"down{layer}"][4 * fb + q]) for q in range(4)]
                for a, b in HALVES:
                    ps, pw, pj = PA.take()
                    tp = mm(ps[:, 0:b - a], [(ws[k // 8][0][:, k % 8, :], FF[:, k, a:b]) for k in range(32)],
                            [x[1] for x in ws], pw, ta)
                    t_h = tt(DV, H[:, fb, a:b], H[:, fb, a:b], ps[:, 0:b - a], ALU.add, tp)
                    PA.give(pj, t_h)
                for x in ws:
                    WR.give(x[2], tp)

        def project_out(name, nk, OG, t_og):
            nonlocal t_h
            for fb in range(8):
                ws = [load(X[name][(nk // 8) * fb + q]) for q in range(nk // 8)]
                for a, b in HALVES:
                    ps, pw, pj = PD.take()
                    tp = mm(ps[:, 0:b - a], [(ws[k // 8][0][:, k % 8, :], OG[:, k, 48 + a:48 + b]) for k in range(nk)],
                            [x[1] for x in ws], pw, t_og)
                    t_h = tt(DV, H[:, fb, a:b], H[:, fb, a:b], ps[:, 0:b - a], ALU.add, tp)
                    PD.give(pj, t_h)
                for x in ws:
                    WR.give(x[2], tp)

        def small_proj(wt_ap, c0, nh, t):
            r = []
            for a, b in HALVES:
                ps, pw, pj = PA.take()
                tp = mm(ps[0:nh, 0:b - a], [(wt_ap[:, k, c0:c0 + nh], hn(k, a, b)) for k in range(8)], pw, t)
                r.append((ps, pj, tp, a, b))
            return r

        t_x = rmsnorm("attn0", XN, HALVES, [t_h, tx], PE.now())
        OG = alloc(16, 576)

        def phase_consts(nh, extra_w, ncol):
            w = alloc(8, ncol)
            t2 = dma(AC, once(), w, X[extra_w].rearrange("p (k f) -> p k f", k=8), [x.now() for x in ENGS])
            return w, t2

        RB = alloc(9, 64)[0:16]
        CUM = alloc(9, 64)[0:16]
        BC = alloc(9, 8)
        NBE = alloc(9, 8)
        CC = alloc(9, 8)
        LC = alloc(9, 8)
        LB = alloc(9, 16)
        work = top[0]
        BAW, t_sw = phase_consts(16, "w_ba", 32)
        RR = [alloc(9, 64)[0:16] for _ in range(3)]
        DUP = Ring([alloc(9, 2, 64)[0:16] for _ in range(2)])
        RST = alloc(576)[0:16]
        NA = alloc(2)
        t_rs = dma(AC, once(), RST, X["reset"][0:16, :])
        t_rs = [t_rs, t_sw]

        def flat_row(r):
            return r.rearrange("p c i -> p (c i)")

        def scan_rows(cum, g, nh, t):
            rst = RST[0:nh]
            return DV.do(lambda e: e.tensor_tensor_scan(flat_row(cum), rst, flat_row(g), 0.0, ALU.mult, ALU.add),
                         t, t_rs)

        def dup_cols(row, nh, dst, t, full=None):
            d, dw, dj = DUP.take()
            t1 = expand(row, d, nh, flat([t, dw]))
            r = to_cols(d.rearrange("p c d i -> p c (d i)"), nh, dst, t1, full)
            DUP.give(dj, r, PE.now())
            return r

        z0 = [mset(PO, RB, 0.0), mset(PO, RR[0], 0.0), mset(PO, RR[1], 0.0)]
        bt = []
        for ps, pj, tp, a, b in small_proj(BAW, 0, 16, [t_sw, t_x]):
            t1 = act(flat_row(RB)[:, 48 + a:48 + b], ps[0:16, 0:b - a], ACT.Sigmoid, tp, z0)
            PA.give(pj, t1)
            bt.append(t1)
        at = []
        for ps, pj, tp, a, b in small_proj(BAW, 16, 16, [t_sw, t_x]):
            t1 = act(flat_row(RR[0])[:, 48 + a:48 + b], ps[0:16, 0:b - a], ACT.Identity, tp, z0,
                     bias=ROWP[0:16, 1:2])
            PA.give(pj, t1)
            at.append(t1)
        t1 = act(NA[0:16, 0:1], ROWP[0:16, 0:1], ACT.Exp)
        t1 = ts(DV, NA[0:16, 1:2], NA[0:16, 0:1], -1.0, None, ALU.mult, None, t1)
        y = flat_row(RR[0])[:, 48:576]
        tmp = flat_row(RR[2])[:, 48:576]
        gsp = flat_row(RR[1])[:, 48:576]
        t2 = log_part(gsp, y, tmp, 16, [at, z0], 1.0)
        t2 = ts(DV, gsp, gsp, NA[0:16, 1:2], None, ALU.mult, None, t1, t2)
        t_cum = scan_rows(CUM, RR[1], 16, t2)
        t3 = tt(PO, RR[0], CUM[:, :, 63:64].to_broadcast([16, 9, 64]), CUM, ALU.subtract, t_cum, t2)
        tc1 = dup_cols(RB, 16, BC, bt)
        tc2 = dup_cols(CUM, 16, CC, t_cum)
        tc3 = dup_cols(RR[0], 16, LC, t3)
        t4 = tcopy(PO, RR[2], CUM[:, :, 63:64].to_broadcast([16, 9, 64]), t_cum, t2)
        tc4 = dup_cols(RR[2], 16, None, t4, LB)
        t5 = act(LC, LC, ACT.Exp, tc3)
        t5 = act(LB, LB, ACT.Exp, tc4)
        t5 = act(NBE, CC, ACT.Exp, tc2)
        t_cols = [t5, stt(NBE, NBE, -1.0, BC, ALU.mult, ALU.mult, t5, tc1)]
        fence()
        top[0] = work

        QD = Ring([alloc(9, 2, 64) for _ in range(2)])
        KD = Ring([alloc(9, 2, 64) for _ in range(2)])
        VD = Ring([alloc(9, 2, 64) for _ in range(2)])
        XC = Ring([alloc(532) for _ in range(1)])
        YC = Ring([alloc(528) for _ in range(1)])
        EC, DD, BB, TA, TB, BV, KE = (alloc(9, 128) for _ in range(7))
        MR = Ring([alloc(3, 128) for _ in range(1)])
        XR = Ring([alloc(3, 128) for _ in range(1)])
        RC = alloc(128)
        VN = alloc(128)
        ST = alloc(2, 128)
        z1 = [mset(PO, b, 0.0) for r in (QD, KD, VD) for b in r.bufs] + [mset(PO, OG, 0.0)]
        z1 = z1 + [mset(PO, b[:, 0:3], 0.0) for b in XC.bufs]
        state = {}

        def proj_gdn(p):
            st = dict(og=[])
            qb, qw, qj = QD.take()
            kb, kw, kj = KD.take()
            vb, vw, vj = VD.take()
            for n in range(6):
                w, wt, wj = load(X["w_gdn"][6 * p + n])
                if n < 4:
                    xc, xw, xj = XC.take()
                toks = []
                for hf, (a, b) in enumerate(HALVES):
                    ps, pw, pj = PD.take()
                    tp = mm(ps[:, 0:b - a], [(w[:, k, :], hn(k, a, b)) for k in range(8)], wt, pw, t_x)
                    if n < 4:
                        t1 = copy(xc[:, 3 + a:3 + b], ps[:, 0:b - a], tp, xw, z1)
                    else:
                        t1 = act(OG[:, 2 * p + n - 4, 48 + a:48 + b], ps[:, 0:b - a], ACT.Silu, tp, z1)
                    PD.give(pj, t1)
                    toks.append(t1)
                    yield 1
                WR.give(wj, tp)
                if n < 4:
                    blk = [p, 8 + p, 16 + 2 * p, 17 + 2 * p][n]
                    yc, yw, yj = YC.take()
                    t2 = ts(DV, yc, xc[:, 3:531], col("conv", 4 * blk + 3), None, ALU.mult, None, toks, yw)
                    for s in (2, 1, 0):
                        t2 = stt(yc, xc[:, s:s + 528], col("conv", 4 * blk + s), yc, ALU.mult, ALU.add, t2)
                    XC.give(xj, t2)
                    if n >= 2:
                        t3 = act(vb[:, 0, n - 2, 48:64], yc[:, 0:16], ACT.Silu, t2, vw, z1)
                        t3 = act(vb[:, 1:9, n - 2, :], yc[:, 16:528].rearrange("p (c i) -> p c i", i=64), ACT.Silu,
                                 t2, vw, z1)
                        YC.give(yj, t3)
                        st["v"] = (vb, vj, t3)
                    else:
                        dst, dw, dj = (qb, qw, qj) if n == 0 else (kb, kw, kj)
                        t3 = act(yc, yc, ACT.Silu, t2)
                        r, rw, rj = RT.take()
                        rt = []
                        for a, b in HALVES:
                            rt.append(inv_rms([yc[:, a:b]], b - a, 1.0, r[:, a:b], ONES, t3, rw))
                        sc = 128.0 ** -0.5 if n == 0 else 1.0
                        for d in range(2):
                            t4 = stt(dst[:, 0, d, 48:64], yc[:, 0:16], sc, r[:, 0:16], ALU.mult, ALU.mult,
                                     rt, dw, z1)
                            t4 = stt(dst[:, 1:9, d, :], yc[:, 16:528].rearrange("p (c i) -> p c i", i=64), sc,
                                     r[:, 16:528].rearrange("p (c i) -> p c i", i=64), ALU.mult, ALU.mult,
                                     rt, dw, z1)
                        YC.give(yj, t4)
                        RT.give(rj, t4)
                        st["qk"[n]] = (dst, dj, t4)
                elif n == 5:
                    st["z"] = t1
                yield 1
            state[p] = st

        t_og = []
        prev = {}

        def three(ap, g):
            return ap[:, 3 * g:3 * g + 3, :]

        def b3(c128):
            return c128.unsqueeze(1).to_broadcast([128, 3, 128])

        def decay(p, g, colsrc, rowtok, h0, rows, dd, ec, q2, free):
            ps, pw, pj = PA.take()
            tp = row_bcast(rows, h0, g, ps, pw, rowtok)
            p3 = ps[:, 0:384].rearrange("p (c x) -> p c x", c=3)
            te = act(three(ec, g), p3, ACT.Exp, tp, free)
            t1 = tt(PO, three(ec, g), three(ec, g), three(q2, g), ALU.mult, te)
            t2 = tt(DV, three(dd, g), p3, colsrc[:, 3 * g:3 * g + 3, p:p + 1].to_broadcast([128, 3, 128]),
                    ALU.subtract, tp, te, free)
            PA.give(pj, t2)
            t2 = tt(PO, three(dd, g), three(dd, g), b3(CS["mask"]), ALU.add, t2)
            t2 = act(three(dd, g), three(dd, g), ACT.Exp, t2)
            return t1, t2

        def pairs3(fn_l, fn_r, g, *after):
            ps, pw, pj = PA.take()
            for n in range(3):
                tp = mm(ps[:, n * 128:(n + 1) * 128], [(fn_l(3 * g + n, n), fn_r(3 * g + n, n))], pw, *after)
            return ps[:, 0:384].rearrange("p (c x) -> p c x", c=3), pj, tp

        def chain_gdn(p):
            st = state[p]
            (q, qj, tq), (k, kj, tk_), (v, vj, tv), tz = st["q"], st["k"], st["v"], st["z"]
            q2, k2, v2 = (x.rearrange("p c h i -> p c (h i)") for x in (q, k, v))
            free = prev.get("done")
            t_att, t_ec, t_ta, t_tb, t_bv, t_ke = {}, {}, {}, {}, {}, {}
            for g in range(3):
                t_ec[g], td = decay(p, g, CC, [t_cum, t_cols, tq], 2 * p, CUM, DD, EC, q2, free)
                psb, pbw, pbj = PA.take()
                tpb = row_bcast(RB, 2 * p, g, psb, pbw, bt)
                pk, pj, tp = pairs3(lambda c, n: k2[:, c, :], lambda c, n: k2[:, c, :], g, tk_)
                t1 = tt(DV, three(BB, g), pk, three(DD, g), ALU.mult, tp, td, free)
                PA.give(pj, t1)
                t1 = tt(DV, three(BB, g), psb[:, 0:384].rearrange("p (c x) -> p c x", c=3), three(BB, g), ALU.mult,
                        t1, tpb)
                PA.give(pbj, t1)
                yield 1
                pk, pj, tp = pairs3(lambda c, n: k2[:, c, :], lambda c, n: q2[:, c, :], g, tq)
                t_att[g] = tt(DV, three(DD, g), pk, three(DD, g), ALU.mult, tp, t1)
                PA.give(pj, t_att[g])
                ps, pw, pj = PA.take()
                for n in range(3):
                    tp = tr(ps[:, n * 128:(n + 1) * 128], v2[:, 3 * g + n, :], tv, pw)
                t_bv[g] = tt(DV, three(BV, g), ps[:, 0:384].rearrange("p (c x) -> p c x", c=3),
                             BC[:, 3 * g:3 * g + 3, p:p + 1].to_broadcast([128, 3, 128]), ALU.mult, tp, free)
                PA.give(pj, t_bv[g])
                ps, pw, pj = PA.take()
                for n in range(3):
                    tp = tr(ps[:, n * 128:(n + 1) * 128], k2[:, 3 * g + n, :], tk_, pw)
                t_ke[g] = tt(DV, three(KE, g), ps[:, 0:384].rearrange("p (c x) -> p c x", c=3),
                             LC[:, 3 * g:3 * g + 3, p:p + 1].to_broadcast([128, 3, 128]), ALU.mult, tp, free)
                PA.give(pj, t_ke[g])
                yield 1
                m, mw, mj = MR.take()
                tm_ = tt(PO, m, three(BB, g), b3(CS["lev0"]), ALU.mult, t1, mw)
                t_tb[g] = tt(PO, three(TB, g), b3(IDENT), m, ALU.subtract, tm_, free)
                px, pj, tp = pairs3(lambda c, n: m[:, n, :], lambda c, n: IDENT, g, tm_)
                t_ta[g] = tt(DV, three(TA, g), b3(IDENT), px, ALU.subtract, tp, free)
                PA.give(pj, t_ta[g])
                MR.give(mj, t_tb[g], tp)
                yield 1
            for lv in range(1, 6):
                for g in range(3):
                    m, mw, mj = MR.take()
                    tm_ = tt(PO, m, three(BB, g), b3(CS[f"lev{lv}"]), ALU.mult, mw)
                    px, pj, tp = pairs3(lambda c, n: m[:, n, :], lambda c, n: TA[:, c, :], g, tm_, t_ta[g])
                    MR.give(mj, tp)
                    x, xw, xj = XR.take()
                    tx_ = copy(x, px, tp, xw)
                    PA.give(pj, tx_)
                    yield 1
                    pt, ptj, tpt = pairs3(lambda c, n: x[:, n, :], lambda c, n: TB[:, c, :], g, tx_, t_tb[g])
                    if lv < 5:
                        pd, pdj, tpd = pairs3(lambda c, n: TB[:, c, :], lambda c, n: x[:, n, :], g, tx_)
                        t_ta[g] = tt(DV, three(TA, g), three(TA, g), pd, ALU.subtract, tpd)
                        PA.give(pdj, t_ta[g])
                    else:
                        tpd = tpt
                    XR.give(xj, tpt, tpd)
                    t_tb[g] = tt(DV, three(TB, g), three(TB, g), pt, ALU.subtract, tpt, tpd)
                    PA.give(ptj, t_tb[g])
                    yield 1
            t_s = mset(PO, ST, 0.0, free)
            t_r = t_v = None
            for c in range(9):
                g = c // 3
                ps, pw, pj = PA.take()
                for d in range(2):
                    tp = mm(ps[d * 64:d * 64 + 64, 0:128], [(k[:, c, d, :], ST[:, d, :])], t_s, pw)
                t_r = stt(RC, ps[:, 0:128], NBE[:, c, p:p + 1], BV[:, c, :], ALU.mult, ALU.add, tp, t_bv[g], t_r)
                PA.give(pj, t_r)
                yield 1
                ps, pw, pj = PA.take()
                tp = mm(ps[:, 0:128], [(TB[:, c, :], RC)], t_r, t_tb[g], pw)
                t_v = copy(VN, ps[:, 0:128], tp, PE.now())
                PA.give(pj, t_v)
                yield 1
                news = []
                po, pow_, poj = PA.take()
                mm(po[:, 0:128], [(VN, DD[:, c, :])], pow_, t_v, t_att[g], t_ec[g], stop=False)
                for d in range(2):
                    tp = mm(po[:, d * 64:d * 64 + 64], [(ST[:, d, :], EC[:, c, d * 64:d * 64 + 64])],
                            start=False, stop=d == 1)
                for d in range(2):
                    ps, pw, pj = PA.take()
                    tps = mm(ps[:, 0:128], [(KE[d * 64:d * 64 + 64, c, :], VN[d * 64:d * 64 + 64, :])], pw, t_ke[g])
                    news.append((ps, pj, tps))
                t_o = copy(v2[:, c, :], po[:, 0:128], tp)
                PA.give(poj, t_o)
                t_s = []
                for d, (ps, pj, tps) in enumerate(news):
                    t = stt(ST[:, d, :], ST[:, d, :], LB[:, c, 2 * p + d:2 * p + d + 1], ps[:, 0:128],
                            ALU.mult, ALU.add, tps, tp)
                    PA.give(pj, t)
                    t_s.append(t)
                yield 1
            done = [t_s, t_o, PE.now()]
            QD.give(qj, done, [t_ec[g] for g in range(3)])
            KD.give(kj, done)
            og = OG[:, 2 * p:2 * p + 2, :].rearrange("p h (c i) -> p c h i", c=9)
            for g in range(3):
                r, rw, rj = RT.take()
                r3 = r[:, 0:384].rearrange("p (c x) -> p c x", c=3)
                t1 = inv_rms([three(v2, g)], 384, 1.0 / 128, r[:, 0:384], ONES, t_o, rw, ring=PA)
                t0 = t1
                t1 = [tt(PO, r3[:, :, d * 64:d * 64 + 64], r3[:, :, d * 64:d * 64 + 64],
                         og[:, 3 * g:3 * g + 3, d, :], ALU.mult, t0, tz) for d in range(2)]
                for d in range(2):
                    t2 = stt(og[:, 3 * g:3 * g + 3, d, :], v[:, 3 * g:3 * g + 3, d, :], col("gdnn"),
                             r3[:, :, d * 64:d * 64 + 64], ALU.mult, ALU.mult, t1)
                RT.give(rj, t2)
                yield 1
            VD.give(vj, t2)
            t_og.append(t2)
            prev["done"] = [done, [x.now() for x in ENGS]]

        for p in range(9):
            weave(proj_gdn(p) if p < 8 else none(), chain_gdn(p - 1) if p else none(), 5)
        project_out("gdn_out", 16, OG, t_og[-1])
        dump("h4", H, t_h)
        ffn(0)
        dump("h5", H, t_h)

        fence()
        top[0] = base
        t_x = rmsnorm("attn1", XN, HALVES, t_h, PE.now())
        OG = alloc(8, 576)
        GWT, t_sw = phase_consts(8, "w_if", 16)
        IR = alloc(9, 64)[0:8]
        CUM = alloc(9, 64)[0:8]
        CC, LC, LB = alloc(9, 4), alloc(9, 4), alloc(9, 4)
        work = top[0]
        RR = [alloc(9, 64)[0:16] for _ in range(3)]
        RR8 = [x[0:8] for x in RR]
        DUP = Ring([alloc(9, 2, 64)[0:16] for _ in range(2)])
        RST = alloc(576)[0:16]
        GBI = alloc(2)
        t_rs = dma(AC, once(), RST, X["reset"][0:16, :])
        t_rs = [t_rs, t_sw]
        tg = ts(DV, GBI[0:8, :], ROWP[0:8, 2:4], 1.0 / 15.0, None, ALU.mult, None)
        z0 = [mset(PO, IR, 0.0), mset(PO, RR[0], 0.0), mset(PO, RR[1], 0.0)]
        ab = []
        for n, dst in ((0, IR), (1, RR8[0])):
            for ps, pj, tp, a, b in small_proj(GWT, 8 * n, 8, [t_sw, t_x]):
                dv = flat_row(dst)[:, 48 + a:48 + b]
                t1 = act(dv, ps[0:8, 0:b - a], ACT.Tanh, tp, z0, tg, bias=GBI[0:8, n:n + 1], scale=1.0 / 15.0)
                PA.give(pj, t1)
                ab.append(ts(DV, dv, dv, 15.0, None, ALU.mult, None, t1))
        y = flat_row(RR8[0])[:, 48:576]
        lf = flat_row(RR8[1])[:, 48:576]
        t2 = log_part(lf, y, flat_row(RR8[2])[:, 48:576], 8, [ab, z0], -1.0)
        t2 = ts(DV, lf, lf, -1.0, None, ALU.mult, None, t2)
        t_cum = scan_rows(CUM, RR8[1], 8, t2)
        t3 = tt(PO, RR8[0], CUM, IR, ALU.subtract, t_cum, ab, t2)
        tc1 = dup_cols(RR8[0], 8, CC, t3)
        t4 = tt(PO, RR8[2], CUM[:, :, 63:64].to_broadcast([8, 9, 64]), RR8[0], ALU.subtract, t3, t2)
        tc2 = dup_cols(RR8[2], 8, LC, t4)
        t4 = tcopy(PO, RR8[1], CUM[:, :, 63:64].to_broadcast([8, 9, 64]), t_cum)
        tc3 = dup_cols(RR8[1], 8, LB, t4)
        t5 = act(LC, LC, ACT.Exp, tc2)
        t_cols = [act(LB, LB, ACT.Exp, tc3, t5), tc1]
        fence()
        top[0] = work

        QD = Ring([alloc(9, 2, 64) for _ in range(2)])
        KD = Ring([alloc(9, 2, 64) for _ in range(2)])
        VD = Ring([alloc(9, 2, 64) for _ in range(2)])
        EC, DD, BV, KE, DEN = (alloc(9, 128) for _ in range(5))
        ST = alloc(256)
        z1 = [mset(PO, b, 0.0) for r in (QD, KD, VD) for b in r.bufs] + [mset(PO, OG, 0.0)]
        state.clear()
        prev.clear()
        t_og = []

        def proj_ml(p):
            st = {}
            bufs = [QD.take(), KD.take(), VD.take()]
            for n in range(6):
                w, wt, wj = load(X["w_ml"][6 * p + n])
                if n < 4:
                    buf, bw, bj = bufs[[0, 1, 2, 2][n]]
                for hf, (a, b) in enumerate(HALVES):
                    ps, pw, pj = PD.take()
                    tp = mm(ps[:, 0:b - a], [(w[:, k, :], hn(k, a, b)) for k in range(8)], wt, pw, t_x)
                    ts_ = []
                    if n >= 4:
                        t1 = act(OG[:, 2 * p + n - 4, 48 + a:48 + b], ps[:, 0:b - a], ACT.Sigmoid, tp, z1)
                        PD.give(pj, t1)
                        st["z"] = t1
                        yield 1
                        continue
                    for lo, hi, cs, is_ in chunks(0, hf):
                        wd = is_.stop - is_.start
                        if n < 2:
                            for d in range(2):
                                pp = slice(d * 64, d * 64 + 64)
                                ts_.append(act(buf[pp, cs, d, is_],
                                               ps[pp, lo:hi].rearrange("p (c i) -> p c i", i=wd),
                                               ACT.Copy, tp, bw, z1, scale=1.0 if n == 0 else 0.125))
                        else:
                            ts_.append(act(buf[:, cs, n % 2, is_], ps[:, lo:hi].rearrange("p (c i) -> p c i", i=wd),
                                           ACT.Copy, tp, bw, z1))
                    PD.give(pj, ts_)
                    st["qkvv"[n]] = (buf, bj, ts_[-1])
                    yield 1
                WR.give(wj, tp)
            state[p] = st

        def chain_ml(p):
            st = state[p]
            (q, qj, tq), (k, kj, tk_), (v, vj, tv), tz = st["q"], st["k"], st["v"], st["z"]
            q2, k2, v2 = (x.rearrange("p c h i -> p c (h i)") for x in (q, k, v))
            free = prev.get("done")
            t_w, t_ec, t_bv, t_ke = {}, {}, {}, {}
            for g in range(3):
                t_ec[g], td = decay(p, g, CC, [t_cum, t_cols, tq], 2 * p, CUM, DD, EC, q2, free)
                yield 1
                pk, pj, tp = pairs3(lambda c, n: k2[:, c, :], lambda c, n: q2[:, c, :], g, tq, tk_)
                t_w[g] = tt(DV, three(DD, g), pk, three(DD, g), ALU.mult, tp, td)
                PA.give(pj, t_w[g])
                ps, pw, pj = PA.take()
                for n in range(3):
                    tp = tr(ps[:, n * 128:(n + 1) * 128], v2[:, 3 * g + n, :], tv, pw)
                t_bv[g] = copy(three(BV, g), ps[:, 0:384].rearrange("p (c x) -> p c x", c=3), tp, free)
                PA.give(pj, t_bv[g])
                ps, pw, pj = PA.take()
                for n in range(3):
                    tp = tr(ps[:, n * 128:(n + 1) * 128], k2[:, 3 * g + n, :], tk_, pw)
                t_ke[g] = tt(DV, three(KE, g), ps[:, 0:384].rearrange("p (c x) -> p c x", c=3),
                             LC[:, 3 * g:3 * g + 3, p:p + 1].to_broadcast([128, 3, 128]), ALU.mult, tp, free)
                PA.give(pj, t_ke[g])
                yield 1
            t_s = mset(PO, ST, 0.0, free)
            for c in range(9):
                g = c // 3
                ps, pw, pj = PA.take()
                tp = mm(ps[:, 0:128], [(BV[:, c, :], DD[:, c, :]), (ST[:, 0:128], EC[:, c, :])],
                        pw, t_s, t_w[g], t_ec[g], t_bv[g])
                tp = mm(ps[:, 128:256], [(ONES, DD[:, c, :]), (ST[:, 128:256], EC[:, c, :])])
                t_n = copy(v2[:, c, :], ps[:, 0:128], tp)
                t_d = act(DEN[:, c, :], ps[:, 128:256], ACT.Abs, tp, free)
                PA.give(pj, t_n, t_d)
                ps, pw, pj = PA.take()
                mm(ps[:, 0:128], [(KE[:, c, :], BV[:, c, :])], pw, t_ke[g])
                tp = mm(ps[:, 128:256], [(KE[:, c, :], ONES)])
                t_s = stt(ST, ST, LB[:, c, p:p + 1], ps[:, 0:256], ALU.mult, ALU.add, tp, t_s)
                PA.give(pj, t_s)
                yield 1
            done = [t_s, PE.now()]
            QD.give(qj, done, [t_ec[g] for g in range(3)])
            KD.give(kj, done)
            og = OG[:, 2 * p:2 * p + 2, :].rearrange("p h (c i) -> p c h i", c=9)
            for g in range(3):
                t1 = ts(DV, three(DEN, g), three(DEN, g), 1.0, None, ALU.max, None, t_d)
                t1 = recip(three(DEN, g), three(DEN, g), t1)
                t1 = tt(DV, three(v2, g), three(v2, g), three(DEN, g), ALU.mult, t1, t_n)
                r, rw, rj = RT.take()
                r3 = r[:, 0:384].rearrange("p (c x) -> p c x", c=3)
                t1 = inv_rms([three(v2, g)], 384, 1.0 / 128, r[:, 0:384], ONES, t1, rw, ring=PA)
                t0 = t1
                t1 = [tt(PO, r3[:, :, d * 64:d * 64 + 64], r3[:, :, d * 64:d * 64 + 64],
                         og[:, 3 * g:3 * g + 3, d, :], ALU.mult, t0, tz) for d in range(2)]
                for d in range(2):
                    t2 = stt(og[:, 3 * g:3 * g + 3, d, :], v[:, 3 * g:3 * g + 3, d, :], col("mln", 2 * p + d),
                             r3[:, :, d * 64:d * 64 + 64], ALU.mult, ALU.mult, t1)
                RT.give(rj, t2)
                yield 1
            VD.give(vj, t2)
            t_og.append(t2)
            prev["done"] = [done, [x.now() for x in ENGS]]

        for p in range(5):
            weave(proj_ml(p) if p < 4 else none(), chain_ml(p - 1) if p else none(), 2)
        project_out("ml_out", 8, OG, t_og[-1])
        dump("h6", H, t_h)
        ffn(1)
        l_o = Line(sem("s_o"))
        to = dma(SP, l_o, out.rearrange("p (k t) -> p k t", k=8), H[:, :, 16:528], t_h)
        SP.items.append((flat([to, t_g, (l_dbg.sem, l_dbg.n) if l_dbg.n else None]), None, None, 0))

        print("items", [len(e.items) for e in (PE, DV, AC, PO, SP)], [e.n for e in (PE, DV, AC, PO)])
        block = ctx.enter_context(nc.Block())
        block.sync(SP.play)
        block.tensor(PE.play)
        block.vector(DV.play)
        block.scalar(AC.play)
        block.gpsimd(PO.play)


def kernel(**inputs):
    import concourse.bacc as bacc
    from concourse.bass_utils import run_bass_kernel_spmd as run

    I = {k: np.asarray(v) for k, v in inputs.items()}

    def c(a):
        return np.ascontiguousarray(a)

    def slabs(w):
        K, F = w.shape
        return c(w.reshape(K // 1024, 8, 128, F // 128, 128).transpose(3, 0, 2, 1, 4)).reshape(-1, 128, 1024)

    def colv(v):
        return v.reshape(-1, 128).T

    arr = {}
    cs = consts()
    arr["cst"] = c(np.concatenate([cs[n] for n in CONST_SMALL], axis=1))
    arr["negdist"] = cs["negdist"]
    arr["reset"] = c(cs["reset"])
    conv = I["gdn_conv_2"][0]
    arr["cols"] = c(np.concatenate([
        colv(I["norm1_w"][0]), colv(I["norm2_w"][0]), colv(I["final_norm_w"]), colv(I["attn_norm_2"][0]),
        colv(I["attn_norm_2"][1]), colv(I["ffn_norm_2"][0]), colv(I["ffn_norm_2"][1]), colv(I["b_gate"][0]),
        conv.reshape(4, 32, 128).transpose(2, 1, 0).reshape(128, 128), colv(I["gdn_norm_2"][0]),
        colv(I["mlstm_norm_2"][0]), colv(I["diff_subln_w"][0])], axis=1))
    gb = I["mlstm_gate_bias_2"][0]
    rows = np.zeros((16, 4), np.float32)
    rows[:, 0], rows[:, 1] = I["gdn_a_log_2"][0], I["gdn_dt_bias_2"][0]
    rows[0:8, 2], rows[0:8, 3] = gb[0:8], gb[8:16]
    arr["rows"] = rows
    arr["x"] = c(I["x"][0].reshape(512, 8, 128).transpose(2, 1, 0)).reshape(128, 4096)
    arr["meta"] = c(I["meta_tokens_2"].reshape(16, 8, 128).transpose(2, 1, 0)).reshape(128, 128)
    rel = np.clip(np.arange(128)[:, None] - (np.arange(512)[None, :] - 384), -128, 128) + 128
    arr["bias"] = c(I["chunk_rel_bias"][0][:, rel].transpose(1, 0, 2)).reshape(128, 4096)
    lq = np.stack([I["diff_lq1"][0], I["diff_lk1"][0], I["diff_lq2"][0], I["diff_lk2"][0]])
    arr["lq"] = c(np.broadcast_to(lq.reshape(1, 256), (128, 256)))
    w = slabs(I["w_in"][0])
    order = [x for h in range(8) for x in (h, 8 + h, 16 + h)] + [x for h in range(4) for x in (24 + h, 28 + h, 32 + h)]
    arr["w_att"] = w[order]
    arr["w_gate"] = w[[x for f in range(8) for x in (36 + f, 44 + f)]]
    arr["w_bd"] = slabs(I["w_branch_diff"][0])
    arr["w_bc"] = c(I["w_branch_chunk"][0].reshape(4, 128, 4, 2, 128).transpose(2, 1, 3, 0, 4)).reshape(4, 128, 1024)
    arr["w_out"] = slabs(I["w_out"][0])
    arr["w_q"] = slabs(I["peer_wq"][0])
    arr["keys"] = c(I["peer_keys"][0].transpose(1, 3, 0, 2)).reshape(128, 1024)
    arr["u"] = c(I["peer_u"][0].reshape(128, 128, 8, 128).transpose(1, 3, 2, 0)).reshape(128, 128, 1024)
    arr["v"] = c(I["peer_v"][0].reshape(128, 128, 1024).transpose(1, 0, 2))
    g = I["gdn_in_2"][0]
    wg = slabs(g[:, 0:6144])
    arr["w_gdn"] = wg[[x for p in range(8) for x in (p, 8 + p, 16 + 2 * p, 17 + 2 * p, 32 + 2 * p, 33 + 2 * p)]]
    arr["w_ba"] = c(g[:, 6144:6176].reshape(8, 128, 32).transpose(1, 0, 2)).reshape(128, 256)
    arr["gdn_out"] = slabs(I["gdn_out_2"][0])
    m = I["mlstm_in_2"][0]
    wm = slabs(m[:, 0:3072])
    arr["w_ml"] = wm[[x for p in range(4) for x in (p, 4 + p, 8 + 2 * p, 9 + 2 * p, 16 + 2 * p, 17 + 2 * p)]]
    arr["w_if"] = c(m[:, 3072:3088].reshape(8, 128, 16).transpose(1, 0, 2)).reshape(128, 128)
    arr["ml_out"] = slabs(I["mlstm_out_2"][0])
    for l in range(2):
        arr[f"up{l}"] = slabs(I["ff_up_2"][l])
        arr[f"down{l}"] = slabs(I["ff_down_2"][l])

    nc = bacc.Bacc("TRN2", target_bir_lowering=False, num_devices=1)
    X = {n: nc.dram_tensor("in_" + n, a.shape, F32, kind="ExternalInput").ap() for n, a in arr.items()}
    out = nc.dram_tensor("out_0", (128, 4096), F32, kind="ExternalOutput").ap()
    scratch = nc.dram_tensor("scratch", (8, 128, 128, 64), F32, kind="Internal").ap()
    dbg = {n: nc.dram_tensor("dbg_" + n, (128,) + s, F32, kind="ExternalOutput").ap() for n, s in DBG}
    build(nc, X, out, scratch, dbg)
    r = run(nc, [{"in_" + n: a for n, a in arr.items()}], core_ids=[0])
    got = r.results[0]["out_0"]
    return c(got.reshape(128, 8, 512).transpose(2, 1, 0)).reshape(1, 512, 1024)
```

```python
from contextlib import ExitStack

import numpy as np
import concourse.bass as bass
from concourse import mybir

ALU = mybir.AluOpType
ACT = mybir.ActivationFunctionType
F32 = mybir.dt.float32
F32R = mybir.dt.float32r
U32 = mybir.dt.uint32
AX = mybir.AxisListType.X

NEG = -1.0e30
RAW = 3
SPLIT = 3
AHEAD = 16
HALVES = [(0, 272), (272, 528)]
DBG = []


class Engine:

    def __init__(self, sem):
        self.sem, self.n, self.items = sem, 0, []

    def do(self, fn, *after):
        self.n += 1
        self.items.append((flat(after), fn, self.sem, 1))
        return (self.sem, self.n)

    def silent(self, fn, *after):
        self.items.append((flat(after), fn, None, 0))

    def dma(self, fn, line, *after):
        line.n += 16
        self.items.append((flat(after), fn, line.sem, 16))
        return (line.sem, line.n)

    def now(self):
        return (self.sem, self.n)

    def play(self, eng):
        seen = {}
        for after, fn, sem, amount in self.items:
            best = {}
            for s, v in after:
                best[s] = max(best.get(s, 0), v)
            for s, v in best.items():
                if v > seen.get(s, 0):
                    eng.wait_ge(s, v)
                    seen[s] = v
            if fn is None:
                continue
            ins = fn(eng)
            if sem is not None:
                ins.then_inc(sem, amount)


class Line:

    def __init__(self, sem):
        self.sem, self.n = sem, 0


class Ring:

    def __init__(self, bufs):
        self.bufs, self.free = bufs, [(j, []) for j in range(len(bufs))]

    def can(self, below=99):
        return any(j < below for j, _ in self.free)

    def take(self, below=99):
        assert self.can(below), "no buffer has been given back"
        n = next(n for n, (j, _) in enumerate(self.free) if j < below)
        j, toks = self.free.pop(n)
        return self.bufs[j], toks, j

    def give(self, j, *toks):
        self.free.append((j, flat(toks)))


def flat(x):
    if x is None:
        return []
    if isinstance(x, list) or (isinstance(x, tuple) and not (len(x) == 2 and isinstance(x[1], int))):
        return [t for y in x for t in flat(y)]
    return [x]


def weave(main, side):
    for k in side:
        for _ in range(k):
            next(main, None)
    for _ in main:
        pass


def plan():
    yield from (("w_att", i) for i in range(36))
    for f in range(8):
        yield from (("w_gate", 2 * f), ("w_gate", 2 * f + 1), ("w_bd", f))
        if f % 2 == 0:
            yield ("w_bc", f // 2)
    yield from (("w_out", i) for i in range(8))
    yield from (("w_q", i) for i in range(8))
    yield from (("u", j) for j in range(4 * AHEAD))
    for i in range(AHEAD):
        c = 4 * (AHEAD + i)
        yield from (("u", c + j) for j in (0, 1))
        if i:
            yield from (("v", c - 4 + j) for j in range(4))
        yield from (("u", c + j) for j in (2, 3))
        yield from (("v", 4 * i + j) for j in range(4))
    yield from (("v", 124 + j) for j in range(4))

    def ffn(layer):
        for half in range(2):
            yield from ((f"up{layer}", 16 * half + i) for i in range(16))
            for fb in range(8):
                yield from ((f"down{layer}", 4 * fb + 2 * half + i) for i in range(2))
    yield from (("w_gdn", i) for i in range(48))
    yield from (("gdn_out", 2 * (i % 8) + i // 8) for i in range(16))
    yield from ffn(0)
    yield from (("w_ml", i) for i in range(24))
    yield from (("ml_out", i) for i in range(8))
    yield from ffn(1)


def consts():
    c = {}
    p = np.arange(128)[:, None]
    f = np.arange(128)[None, :]
    c["ident"] = (p == f).astype(np.float32)
    blk = (p // 64) == (f // 64)
    j, i = p % 64, f % 64
    c["mask"] = np.where(blk & (i >= j), 0.0, NEG).astype(np.float32)
    for n, b in enumerate((1, 2, 4, 8, 16, 32)):
        m = blk & (i // (2 * b) == j // (2 * b)) & (i % (2 * b) >= b) & (j % (2 * b) < b)
        c[f"lev{n}"] = m.astype(np.float32)
    k = np.arange(512)[None, :]
    nd = -np.abs(p - (k - 384)).astype(np.float32)
    nd[0:64, 448:512] = NEG
    c["negdist"] = nd
    c["iota"] = np.broadcast_to(f, (128, 128)).astype(np.float32)
    c["reset"] = np.broadcast_to((np.arange(576) % 64 != 0), (128, 576)).astype(np.float32)
    return c


CONST_SMALL = ["ident", "mask", "lev0", "lev1", "lev2", "lev3", "lev4", "lev5", "iota"]
COLS = dict(norm1=(0, 8), norm2=(8, 8), final=(16, 8), attn0=(24, 8), attn1=(32, 8), ffn0=(40, 8), ffn1=(48, 8),
            bgate=(56, 16), conv=(72, 128), gdnn=(200, 1), mln=(201, 8), subln=(209, 1))


def build(nc, X, out, scratch, scratch2, dbg):
    ctx = ExitStack()
    with ctx:
        def sem(name):
            return ctx.enter_context(nc.semaphore(name))

        base_at = (nc.sbuf_base + 63) // 64 * 64
        NCOL = (nc.sbuf_usable_end - base_at) // 4 - 64
        ctx.enter_context(nc.sbuf_tensor("slab", [128, NCOL + 16], F32))
        banks = [ctx.enter_context(nc.psum_tensor(f"bank{i}", [128, 512], F32)) for i in range(8)]

        PE, DV, AC, PO, SP = (Engine(sem(n)) for n in ("s_pe", "s_dv", "s_ac", "s_po", "s_sp"))
        ENGS = (PE, DV, AC, PO)

        top = [0]

        n_alloc = [0]

        def alloc(*dims, dt=F32):
            n = int(np.prod(dims))
            o = top[0]
            top[0] += n
            assert top[0] <= NCOL, (top[0], NCOL)
            n_alloc[0] += 1
            a = nc.alloc_sbuf_tensor_at(f"t{n_alloc[0]}", [128, n], dt, offset=base_at + 4 * o, align_bytes=4)[:, :]
            if len(dims) == 2:
                return a.rearrange("p (a b) -> p a b", a=dims[0])
            if len(dims) == 3:
                return a.rearrange("p (a b c) -> p a b c", a=dims[0], b=dims[1])
            return a

        def alloc2(*dims):
            return alloc(*dims, dt=F32R), alloc(*dims, dt=F32R)

        def fence(*also):
            toks = flat([[e.now() for e in ENGS], also])
            for e in ENGS:
                e.items.append((toks, None, None, 0))
            return toks

        def act(out, in_, func, *after, bias=None, scale=1.0, accum=None):
            kw = dict(scale=scale)
            if bias is not None:
                kw["bias"] = bias
            if accum is not None:
                kw["accum_out"] = accum
            return AC.do(lambda e: e.activation(out, in_, func, **kw), *after)

        def copy(out, in_, *after):
            return AC.do(lambda e: e.activation(out, in_, ACT.Copy), *after)

        def tt(E, out, a, b, op, *after):
            return E.do(lambda e: e.tensor_tensor(out, a, b, op), *after)

        def ts(E, out, a, s1, s2, op0, op1, *after):
            if op1 is None:
                return E.do(lambda e: e.tensor_scalar(out, a, s1, None, op0), *after)
            return E.do(lambda e: e.tensor_scalar(out, a, s1, s2, op0, op1), *after)

        def stt(out, a, s, b, op0, op1, *after):
            return DV.do(lambda e: e.scalar_tensor_tensor(out=out, in0=a, scalar=s, in1=b, op0=op0, op1=op1), *after)

        def recip(out, in_, *after):
            return DV.do(lambda e: e.reciprocal(out, in_), *after)

        def tcopy(E, out, in_, *after):
            return E.do(lambda e: e.tensor_copy(out, in_), *after)

        def reduce(out, in_, op, *after):
            return DV.do(lambda e: e.tensor_reduce(out=out, in_=in_, op=op, axis=AX), *after)

        def dma(E, line, out, in_, *after):
            return E.dma(lambda e: e.dma_start(out, in_), line, *after)

        def mset(E, out, v, *after):
            return E.do(lambda e: e.memset(out, v), *after)

        def mm(out, terms, *after, start=True, stop=True):
            tok = None
            for i, (l, r) in enumerate(terms):
                s0, s1 = start and i == 0, stop and i == len(terms) - 1

                def fn(e, l=l, r=r, s0=s0, s1=s1):
                    return e.matmul(out, l, r, start=s0, stop=s1)
                if i == len(terms) - 1:
                    tok = PE.do(fn, *(after if i == 0 else ()))
                else:
                    PE.silent(fn, *(after if i == 0 else ()))
            return tok

        def tr(out, in_, *after):
            return PE.do(lambda e: e.transpose(out, in_, IDENT), *after)

        def split(src, hi, lo, *after, E=None):
            t1 = copy(hi, src, *after)
            return [t1, tt(E or DV, lo, src, hi.bitcast(F32), ALU.subtract, t1)]

        def terms3(wh, wl, xh, xl):
            return [(wh, xh), (wh, xl), (wl, xh)]

        lines = [Line(sem(f"s_w{i}")) for i in range(5)]
        RAWR = Ring([alloc(1024) for _ in range(RAW)])
        WS = Ring([alloc2(8, 128) for _ in range(SPLIT)])
        todo = list(plan())
        arriving, ready = [], []
        n_split = [0]

        room = {}

        def send():
            while todo and RAWR.can(room.get(todo[0][0], (RAW, 0))[0]):
                buf, free, j = RAWR.take(room.get(todo[0][0], (RAW, 0))[0])
                name, i = todo.pop(0)
                arriving.append((name, i, buf, dma(SP, lines[j], buf, X[name][i], free), j))

        def prepare():
            while arriving and WS.can(room.get(arriving[0][0], (0, SPLIT))[1]):
                name, i, buf, t, j = arriving.pop(0)
                (hi, lo), free, wj = WS.take(room.get(name, (0, SPLIT))[1])
                E = PO if n_split[0] % 3 == 2 or name == "u" and i < 4 * AHEAD else DV
                n_split[0] += 1
                b3_ = buf.rearrange("p (k f) -> p k f", f=128)
                parts = 4 if name in ("w_gdn", "w_ml") else 8
                toks = [split(b3_[:, k:k + parts, :], hi[:, k:k + parts, :], lo[:, k:k + parts, :], t, free, E=E)
                        for k in range(0, 8, parts)]
                RAWR.give(j, toks)
                ready.append((name, i, hi, lo, toks, wj))
                send()

        def more_room(names, n_raw, n_split_, toks):
            del RAWR.bufs[RAW:], WS.bufs[SPLIT:]
            RAWR.free = [x for x in RAWR.free if x[0] < RAW]
            WS.free = [x for x in WS.free if x[0] < SPLIT]
            for i in range(n_raw):
                RAWR.bufs.append(alloc(1024))
                RAWR.free.append((RAW + i, toks))
            for i in range(n_split_):
                WS.bufs.append(alloc2(8, 128))
                WS.free.append((SPLIT + i, toks))
            for n in names:
                room[n] = (RAW + n_raw, SPLIT + n_split_)
            send()
            prepare()

        def slab(name, i):
            if not ready:
                send()
                prepare()
            nm, k, hi, lo, toks, wj = ready.pop(0)
            assert (nm, k) == (name, i), (nm, k, name, i)
            return hi, lo, toks, wj

        def done_with(wj, tok):
            WS.give(wj, tok)
            prepare()

        l_c = Line(sem("s_c"))
        n_once = [0]

        def once():
            n_once[0] += 1
            return Line(sem(f"s_once{n_once[0]}"))

        CS = {}
        for n in CONST_SMALL:
            CS[n] = alloc(128)
        CB_ = alloc(210)
        ROWP = alloc(8)
        ct = []
        for i, n in enumerate(CONST_SMALL):
            ct.append(dma(AC, l_c, CS[n], X["cst"][:, i * 128:(i + 1) * 128]))
        ct.append(dma(AC, l_c, CB_, X["cols"][:, :]))
        ct.append(dma(AC, l_c, ROWP[0:16, 0:4], X["rows"][:, :]))
        C0 = ct[-1]
        IDENT = CS["ident"]
        ONES = alloc(128)
        ONE = ONES[:, 0:1]
        EPS = alloc(1)
        t = [mset(PO, ONES, 1.0), mset(PO, EPS, 1e-6)]
        K0 = [C0, t]
        for e in (PE, DV, AC, PO):
            e.items.append((flat(K0), None, None, 0))

        def col(name, i=0):
            return CB_[:, COLS[name][0] + i:COLS[name][0] + i + 1]

        PD = Ring([banks[i][:, :] for i in range(3)])
        PA = Ring([banks[i][:, :] for i in range(3, 8)])

        H = alloc(8, 528)
        XH, XL = alloc2(8, 528)
        SQ = Ring([alloc(512) for _ in range(2)])
        RT = Ring([alloc(528) for _ in range(2)])
        base = top[0]
        send()
        prepare()

        l_x = Line(sem("s_x"))
        tx = dma(AC, l_x, H[:, :, 16:528], X["x"].rearrange("p (k t) -> p k t", k=8))
        tm = dma(AC, l_x, H[:, :, 0:16], X["meta"].rearrange("p (k t) -> p k t", k=8))
        tx = [tx, tm]

        def dump(name, ap, *after):
            if name in dbg:
                t = dma(AC, l_dbg, dbg[name], ap, *after)
                for e in (PE, DV, AC, PO, SP):
                    e.items.append(([t], None, None, 0))

        l_dbg = Line(sem("s_dbg"))

        def inv_rms(parts, n, scale, R, lhs, *after, bias=True, ring=None):
            ring = ring or PD
            ps, pw, pj = ring.take()
            for i, a in enumerate(parts):
                sq, sw, sj = SQ.take()
                t1 = act(sq[:, 0:n], a, ACT.Square, sw, *after)
                t2 = mm(ps[:, 0:n], [(lhs, sq[:, 0:n])], t1, pw if i == 0 else None,
                        start=i == 0, stop=i == len(parts) - 1)
                SQ.give(sj, t2)
            t3 = act(R, ps[:, 0:n], ACT.Sqrt, t2, bias=EPS, scale=scale)
            ring.give(pj, t3)
            return recip(R, R, t3)

        def rmsnorm(wname, halves, src_tok, free, dst=None):
            toks = {}
            for a, b in halves:
                r, rw, rj = RT.take()
                n = b - a
                t = inv_rms([H[:, k, a:b] for k in range(8)], n, 1.0 / 1024, r[:, 0:n], ONES, src_tok, rw)
                for k in range(8):
                    if dst is not None:
                        t2 = stt(dst[:, k, a:b], H[:, k, a:b], col(wname, k), r[:, 0:n], ALU.mult, ALU.mult, t, free)
                        toks[a, k] = t2
                    else:
                        q, qw, qj = SQ.take()
                        t2 = stt(q[:, 0:n], H[:, k, a:b], col(wname, k), r[:, 0:n], ALU.mult, ALU.mult, t, qw)
                        t3 = split(q[:, 0:n], XH[:, k, a:b], XL[:, k, a:b], t2, free)
                        SQ.give(qj, t3)
                        toks[a, k] = t3
                RT.give(rj, t2)
            if dst is not None:
                return list(toks.values())
            return lambda a, k=7: toks[max(x for x, _ in toks if x <= a), k]

        def dense(out, w3, x3, *after, n=None, by_k=None):
            wh, wl = w3
            xh, xl = x3
            n = n or 8
            for k in range(n):
                t = mm(out, terms3(wh(k), wl(k), xh(k), xl(k)), *(after if k == 0 else ()), by_k and by_k(k),
                       start=k == 0, stop=k == n - 1)
                if k < n - 1:
                    yield 1
            dense_tok[0] = t

        dense_tok = [None]

        def dense_now(*a, **kw):
            for _ in dense(*a, **kw):
                pass
            return dense_tok[0]

        def by_slab(hi, lo, o=0):
            return (lambda k: hi[:, o + k, :], lambda k: lo[:, o + k, :])

        def of_x(a, b):
            return (lambda k: XH[:, k, a:b], lambda k: XL[:, k, a:b])

        ODH, ODL = alloc2(8, 512)
        OCH, OCL = alloc2(4, 512)
        att_base = top[0]
        BIASR = Ring([alloc(2, 512) for _ in range(2)])
        ND = alloc(512)
        tb = dma(AC, once(), ND, X["negdist"][:, :])
        LQ = alloc(4, 64)
        tb3 = dma(AC, once(), LQ, X["lq"].rearrange("p (k t) -> p k t", k=4))
        LAM = alloc(8)
        LP = alloc(2, 64)
        t = tt(DV, LP[:, 0, :], LQ[:, 0, :], LQ[:, 1, :], ALU.mult, tb3)
        t = tt(DV, LP[:, 1, :], LQ[:, 2, :], LQ[:, 3, :], ALU.mult, tb3)
        t = reduce(LAM[:, 0:2], LP, ALU.add, t)
        t = act(LAM[:, 2:4], LAM[:, 0:2], ACT.Exp, t)
        t = tt(DV, LAM[:, 4:5], LAM[:, 2:3], LAM[:, 3:4], ALU.subtract, t)
        t_lam = ts(DV, LAM[:, 5:6], LAM[:, 4:5], 0.8 - 0.6, -1.0, ALU.add, ALU.mult, t)
        SUB = LAM[:, 6:7]
        t_sub = ts(DV, SUB, col("subln"), 1.0 - (0.8 - 0.6), None, ALU.mult, None, t_lam)

        t_xn = rmsnorm("norm1", [(16, 528)], tx, None)

        QT = Ring([alloc(512) for _ in range(4)])
        KT = Ring([alloc(512) for _ in range(4)])
        VT = Ring([alloc(4, 128) for _ in range(4)])
        S1 = Ring([alloc(512) for _ in range(8)])
        AT = Ring([alloc(512) for _ in range(3)])
        SC = Ring([alloc(8) for _ in range(12)])
        OO = Ring([alloc(512) for _ in range(1)])
        attn_out = {}
        unit = {}

        def proj_all():
            for u in range(12):
                st = {}
                for kind in range(3):
                    wh, wl, wt, wj = slab("w_att", 3 * u + kind)
                    r = (QT, KT, VT)[kind]
                    while not r.free:
                        yield 1
                    b, bw, bj = r.take()
                    ps, pw, pj = PD.take()
                    if kind < 2:
                        yield from dense(ps, by_slab(wh, wl), of_x(16, 528), wt, pw,
                                         by_k=lambda k: t_xn(16, k))
                        tp = dense_tok[0]
                        te = copy(b, ps, tp, bw)
                    else:
                        for tl in range(4):
                            yield from dense(ps[:, tl * 128:(tl + 1) * 128], of_x(16 + tl * 128, 144 + tl * 128),
                                             by_slab(wh, wl), wt, pw, by_k=lambda k: t_xn(16, k))
                            tp = dense_tok[0]
                        te = copy(b, ps.rearrange("p (a b) -> p a b", a=4), tp, bw)
                    st["qkv"[kind]] = (b, te, bj)
                    PD.give(pj, te)
                    done_with(wj, tp)
                    yield 1
                unit[u] = st

        def attend(u):
            st = unit[u]
            (q, qt, qj), (k, kt, kj), (v, vt, vj) = st["q"], st["k"], st["v"]
            diff = u < 8
            po, pow_, poj = PA.take()
            kept, t_bu = {}, [None]
            if not diff:
                bias, bbw, bbj = BIASR.take()
                t_bias = dma(PO, once(), bias, X["bias"][:, (u - 8) * 1024:(u - 7) * 1024]
                             .rearrange("p (k t) -> p k t", k=2), bbw)
                t_bias = mset(PO, bias[0:64, :, 448:512], NEG, t_bias)

            def scores(i):
                N = 128 * (i + 1)
                probs = []
                for m in range(2):
                    lo = m * 64
                    ps, pw, pj = PA.take()
                    tp = mm(ps[:, 0:N], [(q[lo:lo + 64, i * 128:(i + 1) * 128], k[lo:lo + 64, 0:N])],
                            qt, kt, pw)
                    s, sw, sj = S1.take()
                    c, cw, cj = SC.take()
                    if diff:
                        slope = 2.0 ** (-(u + 1))
                        t1 = stt(s[:, 0:N], ND[:, 512 - N:512], slope * 8.0, ps[:, 0:N], ALU.mult, ALU.add,
                                 tp, sw, tb)
                        sc = 0.125
                    else:
                        t1 = stt(s[:, 0:N], ps[:, 0:N], 0.125, bias[:, m, 512 - N:512],
                                 ALU.mult, ALU.add, tp, sw, t_bias)
                        t_bu[0] = t1
                        sc = 1.0
                    PA.give(pj, t1)
                    probs.append([s, sj, c, cj, t1, cw, sc])
                for x in probs:
                    x[4] = reduce(x[2][:, 0:1], x[0][:, 0:N], ALU.max, x[4], x[5])
                for x in probs:
                    x[4] = ts(DV, x[2][:, 1:2], x[2][:, 0:1], -x[6], None, ALU.mult, None, x[4])
                for x in probs:
                    s, c = x[0], x[2]
                    x[4] = act(s[:, 0:N], s[:, 0:N], ACT.Exp, x[4], bias=c[:, 1:2], scale=x[6], accum=c[:, 2:3])
                kept[i] = probs

            def weigh(i):
                N = 128 * (i + 1)
                probs = kept.pop(i)
                for x in probs:
                    x[4] = recip(x[2][:, 3:4], x[2][:, 2:3], x[4])
                (s1, j1, c1, d1, t1, _, _), (s2, j2, c2, d2, t2, _, _) = probs
                if diff:
                    t = tt(DV, c2[:, 4:5], c2[:, 3:4], LAM[:, 5:6], ALU.mult, t2, t_lam)
                    t = ts(DV, s2[:, 0:N], s2[:, 0:N], c2[:, 4:5], None, ALU.mult, None, t)
                    t = stt(s1[:, 0:N], s1[:, 0:N], c1[:, 3:4], s2[:, 0:N], ALU.mult, ALU.add, t, t1)
                    S1.give(j2, t)
                    SC.give(d1, t)
                    SC.give(d2, t)
                    return [(s1, j1, t, 0)]
                ta = ts(DV, s1[:, 0:N], s1[:, 0:N], c1[:, 3:4], None, ALU.mult, None, t1)
                tb_ = ts(DV, s2[:, 0:N], s2[:, 0:N], c2[:, 3:4], None, ALU.mult, None, t2)
                SC.give(d1, ta)
                SC.give(d2, tb_)
                return [(s1, j1, ta, 0), (s2, j2, tb_, 1)]

            def transposed(i, s, sj, t):
                N = 128 * (i + 1)
                ps, pw, pj = PA.take()
                for n in range(i + 1):
                    tp = tr(ps[:, n * 128:(n + 1) * 128], s[:, n * 128:(n + 1) * 128], t, pw)
                S1.give(sj, tp)
                a, aw, aj = AT.take()
                te = copy(a[:, 0:N], ps[:, 0:N], tp, aw)
                PA.give(pj, te)
                return a, aj, te

            def values(i, m, a, aj, te):
                if diff:
                    o, vs = po[:, i * 128:(i + 1) * 128], lambda n: v[:, n, :]
                else:
                    o = po[m * 64:m * 64 + 64, i * 128:(i + 1) * 128]
                    vs = lambda n: v[:, n, m * 64:m * 64 + 64]
                t = mm(o, [(vs(n), a[:, n * 128:(n + 1) * 128]) for n in range(i + 1)], te, vt, pow_)
                AT.give(aj, t)
                return t

            scores(0)
            yield 2
            for i in range(4):
                ws = weigh(i)
                yield 2
                if i < 3:
                    scores(i + 1)
                    yield 3
                for s, sj, t, m in ws:
                    a = transposed(i, s, sj, t)
                    yield 3
                    t_last = values(i, m, *a)
                    yield 2
            QT.give(qj, t_last)
            KT.give(kj, t_last)
            VT.give(vj, t_last)
            o, ow, oj = OO.take()
            t1 = copy(o, po, t_last, ow)
            PA.give(poj, t1)
            if diff:
                yield 2
                r, rw, rj = RT.take()
                t2 = inv_rms([o], 512, 1.0 / 128, r[:, 0:512], ONES, t1, rw, ring=PA)
                t1 = stt(o, o, SUB, r[:, 0:512], ALU.mult, ALU.mult, t2, t_sub)
                RT.give(rj, t1)
                attn_out[u] = split(o, ODH[:, u, :], ODL[:, u, :], t1)
            else:
                BIASR.give(bbj, t_bu[0])
                attn_out[u] = split(o, OCH[:, u - 8, :], OCL[:, u - 8, :], t1)
            OO.give(oj, attn_out[u])
            yield 1

        def attend_all():
            active, u = [], 0
            while active or u < 12:
                while len(active) < 2 and u in unit:
                    active.append(attend(u))
                    u += 1
                if not active:
                    yield 1
                for g in list(active):
                    k = next(g, None)
                    if k is None:
                        active.remove(g)
                    else:
                        yield (k + 1) // 2

        weave(proj_all(), attend_all())

        fence()
        top[0] = att_base
        MGH, MGL = alloc2(8, 512)
        G1 = Ring([alloc(512) for _ in range(4)])
        t_d, t_c = attn_out[7], attn_out[11]
        t_mg = []
        for fb in range(8):
            gs = []
            for n in range(2):
                wh, wl, wt, wj = slab("w_gate", 2 * fb + n)
                ps, pw, pj = PD.take()
                tp = dense_now(ps, by_slab(wh, wl), of_x(16, 528), wt, pw)
                done_with(wj, tp)
                g, gw, gj = G1.take()
                t1 = act(g, ps, ACT.Sigmoid, tp, gw, bias=col("bgate", 8 * n + fb))
                PD.give(pj, t1)
                gs.append((g, gj, t1))
            wh, wl, wt, wj = slab("w_bd", fb)
            ps, pw, pj = PD.take()
            tp = dense_now(ps, by_slab(wh, wl), (lambda k: ODH[:, k, :], lambda k: ODL[:, k, :]), wt, pw, t_d)
            done_with(wj, tp)
            g, gj, tg = gs[0]
            ta = tt(DV, g, g, ps, ALU.mult, tp, tg)
            PD.give(pj, ta)
            if fb % 2 == 0:
                wc = slab("w_bc", fb // 2)
            ps, pw, pj = PD.take()
            tp = dense_now(ps, by_slab(wc[0], wc[1], 4 * (fb % 2)),
                           (lambda k: OCH[:, k, :], lambda k: OCL[:, k, :]), wc[2], pw, t_c, n=4)
            if fb % 2:
                done_with(wc[3], tp)
            g2, gj2, tg2 = gs[1]
            tb_ = tt(DV, g2, g2, ps, ALU.mult, tp, tg2)
            PD.give(pj, tb_)
            t = tt(DV, g, g, g2, ALU.add, tb_, ta)
            t = split(g, MGH[:, fb, :], MGL[:, fb, :], t)
            t_mg.append(t)
            G1.give(gj, t)
            G1.give(gj2, t)
        t_h = None
        for fb in range(8):
            wh, wl, wt, wj = slab("w_out", fb)
            ps, pw, pj = PD.take()
            tp = dense_now(ps, by_slab(wh, wl), (lambda k: MGH[:, k, :], lambda k: MGL[:, k, :]), wt, pw, t_mg[-1])
            done_with(wj, tp)
            t_h = tt(DV, H[:, fb, 16:528], H[:, fb, 16:528], ps, ALU.add, tp)
            PD.give(pj, t_h)
        dump("h1", H, t_h)

        fence()
        top[0] = base
        AF = Ring([alloc(512) for _ in range(4)])
        l_f = [Line(sem(f"s_f{i}")) for i in range(4)]
        t_xn = rmsnorm("norm2", [(16, 528)], t_h, PE.now())
        TT_ = alloc(3, 512)
        after_tt = top[0]
        spilled = {}

        def neurons_ahead():
            for j in range(4 * AHEAD):
                wh, wl, wt, wj = slab("u", j)
                ps, pw, pj = PD.take()
                yield from dense(ps, by_slab(wh, wl), of_x(16, 528), wt, pw)
                tp = dense_tok[0]
                done_with(wj, tp)
                f, fw, fj = AF.take()
                t1 = act(f, ps, ACT.Gelu, tp, fw)
                PD.give(pj, t1)
                spilled[j] = dma(AC, l_f[fj], scratch2[j], f, t1)
                AF.give(fj, spilled[j])
                yield 1

        KEY = alloc(8, 128)
        tk = dma(AC, once(), KEY, X["keys"].rearrange("p (k t) -> p k t", k=8),
                 DV.now(), PE.now(), PO.now())
        QP = alloc(8, 512)
        t_q = None
        for h in range(8):
            wh, wl, wt, wj = slab("w_q", h)
            ps, pw, pj = PD.take()
            tp = dense_now(ps, by_slab(wh, wl), of_x(16, 528), wt, pw, by_k=lambda k: t_xn(16, k))
            done_with(wj, tp)
            t_q = copy(QP[:, h, :], ps, tp)
            PD.give(pj, t_q)
        SS = Ring([alloc(16, 128)])
        S2 = Ring([alloc(256) for _ in range(8)])
        VV = alloc(2, 8, 16)
        II = alloc(2, 8, 16)
        IF = alloc(2, 8, 16)
        CA = alloc(8, 256)
        CV = alloc(8, 16)
        CI = alloc(8, 16)
        AB = alloc(2, 128)
        ABF = alloc(2, 128)
        EQ = alloc(128, 16)
        TK = alloc(3, 128)
        RS = alloc(16)
        iota16 = CS["iota"][:, 0:16]
        t_g = []

        def select():
            nonlocal t_g
            t_sel = {}
            t_selc = None
            for tl in range(4):
                ss, sw, sj = SS.take()
                for s in range(2):
                    for hh in range(2):
                        ps, pw, pj = PA.take()
                        for h in range(4):
                            tp = mm(ps[:, h * 128:(h + 1) * 128],
                                    [(QP[s * 64:s * 64 + 64, 4 * hh + h, tl * 128:(tl + 1) * 128],
                                      KEY[s * 64:s * 64 + 64, 4 * hh + h, :])], t_q, tk, pw)
                        yield 1
                        a0 = s * 8 + hh * 4
                        te = copy(ss[:, a0:a0 + 4, :], ps.rearrange("p (a b) -> p a b", a=4), tp, sw)
                        PA.give(pj, te)

                def top16(n, jobs, t):
                    def idx(i):
                        return i.bitcast(U32)
                    s2 = [S2.take() for _ in jobs]
                    a, b, c, d = [], [], [], []
                    for src, v, i in jobs:
                        a.append(DV.do(lambda e, v=v, src=src: e.max(v[:, 0:8], src), t))
                    for (src, v, i), x in zip(jobs, a):
                        DV.do(lambda e, v=v, i=i, src=src: e.max_index(idx(i[:, 0:8]), v[:, 0:8], src), x)
                    for (src, v, i), (r, rw, _), x in zip(jobs, s2, a):
                        b.append(DV.do(lambda e, v=v, r=r, src=src: e.match_replace(
                            out=r[:, 0:n], in_to_replace=v[:, 0:8], in_values=src, imm_value=-3.0e38), x, rw))
                    for (src, v, i), (r, _, _), x in zip(jobs, s2, b):
                        c.append(DV.do(lambda e, v=v, r=r: e.max(v[:, 8:16], r[:, 0:n]), x))
                    for (src, v, i), (r, _, _), x in zip(jobs, s2, c):
                        d.append(DV.do(lambda e, v=v, i=i, r=r: e.max_index(idx(i[:, 8:16]), v[:, 8:16], r[:, 0:n]), x))
                    for (_, _, rj), x in zip(s2, d):
                        S2.give(rj, x)
                    return d[-1]

                for s in range(2):
                    t = top16(128, [(ss[:, s * 8 + h, :], VV[:, s, h, :], II[:, s, h, :]) for h in range(8)], te)
                    yield 15
                SS.give(sj, t)
                t1 = tcopy(DV, IF, II.bitcast(U32), t)
                t = tt(DV, CA.rearrange("p h (a b) -> p h a b", a=16),
                       VV[:, 0, :, :].unsqueeze(3).to_broadcast([128, 8, 16, 16]),
                       VV[:, 1, :, :].unsqueeze(2).to_broadcast([128, 8, 16, 16]), ALU.add, t1)
                t = top16(256, [(CA[:, h, :], CV[:, h, :], CI[:, h, :]) for h in range(8)], t)
                yield 22
                CIu = CI.rearrange("p a b -> p (a b)").bitcast(U32)
                t1 = ts(DV, AB[:, 0, :].bitcast(U32), CIu, 4, None, ALU.logical_shift_right, None, t)
                t2 = ts(DV, AB[:, 1, :].bitcast(U32), CIu, 15, None, ALU.bitwise_and, None, t)
                t3 = tcopy(DV, ABF, AB.bitcast(U32), t1, t2)
                for s in range(2):
                    t4 = tt(DV, EQ, ABF[:, s, :].unsqueeze(2).to_broadcast([128, 128, 16]),
                            iota16.unsqueeze(1).to_broadcast([128, 128, 16]), ALU.is_equal, t3)
                    e4 = EQ.rearrange("p (h k) a -> p h k a", h=8)
                    t4 = tt(DV, e4, e4, IF[:, s, :, :].unsqueeze(2).to_broadcast([128, 8, 16, 16]), ALU.mult, t4)
                    t3 = reduce(TK[:, s, :], EQ, ALU.add, t4, t_sel.get(tl - 1))
                    yield 9
                G3 = TK[:, 2, :].rearrange("p (h k) -> p h k", h=8)
                MX = RS[:, 8:16]
                t4 = tcopy(DV, MX, CV[:, :, 0:1].rearrange("p a b -> p (a b)"), t3)
                t4 = tt(DV, CV, CV, MX.unsqueeze(2).to_broadcast([128, 8, 16]), ALU.subtract, t4)
                t5 = act(G3, CV, ACT.Exp, t4)
                t5 = reduce(RS[:, 0:8], G3, ALU.add, t5)
                t5 = recip(RS[:, 0:8], RS[:, 0:8], t5)
                t5 = tt(DV, G3, G3, RS[:, 0:8].unsqueeze(2).to_broadcast([128, 8, 16]), ALU.mult, t5)
                ps, pw, pj = PA.take()
                for n in range(3):
                    tp = tr(ps[:, n * 128:(n + 1) * 128], TK[:, n, :], t5, pw)
                te = copy(TT_[:, :, tl * 128:(tl + 1) * 128], ps[:, 0:384].rearrange("p (a b) -> p a b", a=3), tp)
                PA.give(pj, te)
                t_sel[tl] = tp
                t_selc = te
            dump("tt", TT_, t_selc)
            fence()
            top[0] = after_tt
            OH1 = Ring([alloc(8, 128) for _ in range(2)])
            OH2 = Ring([alloc(8, 128) for _ in range(2)])
            GB = Ring([alloc(128, 64) for _ in range(2)])
            l_g = [Line(sem("s_g0")), Line(sem("s_g1"))]
            iota = CS["iota"]
            t_g = []
            for tb_i in range(8):
                gb, gbw, gbj = GB.take()
                for q8 in range(8):
                    t0 = tb_i * 64 + q8 * 8
                    o1, w1, j1 = OH1.take()
                    o2, w2, j2 = OH2.take()
                    ta = tt(DV, o1, iota.unsqueeze(1).to_broadcast([128, 8, 128]),
                            TT_[:, 0, t0:t0 + 8].unsqueeze(2).to_broadcast([128, 8, 128]), ALU.is_equal, t_selc, w1)
                    for n in range(8):
                        tb_ = ts(DV, o2[:, n, :], iota, TT_[:, 1, t0 + n:t0 + n + 1], TT_[:, 2, t0 + n:t0 + n + 1],
                                 ALU.is_equal, ALU.mult, t_selc, w2)
                    for q in range(2):
                        ps, pw, pj = PA.take()
                        for n in range(4):
                            tp = mm(ps[:, n * 128:(n + 1) * 128], [(o1[:, 4 * q + n, :], o2[:, 4 * q + n, :])],
                                    ta, tb_, pw)
                        c0 = q8 * 8 + q * 4
                        te = copy(gb[:, :, c0:c0 + 4].rearrange("p b t -> p t b"),
                                  ps.rearrange("p (t b) -> p t b", t=4), tp, gbw)
                        PA.give(pj, te)
                    yield 2
                    OH1.give(j1, tp)
                    OH2.give(j2, tp)
                td = dma(PO, l_g[gbj], scratch[tb_i], gb, te)
                GB.give(gbj, td)
                t_g.append(td)


        weave(neurons_ahead(), select())
        fz = fence(t_g, list(spilled.values()))
        top[0] = base
        GJ = Ring([alloc(8, 4, 64) for _ in range(2)])
        AA = Ring([alloc2(4, 512) for _ in range(2)])
        AF = Ring([alloc(512) for _ in range(3)])
        FS = Ring([alloc(4, 512)])
        more_room(("u", "v"), 2, 3, fz)
        l_j = [Line(sem("s_j0")), Line(sem("s_j1"))]
        l_fs = Line(sem("s_fs"))

        def weights_of(g):
            gj, gw, gjj = GJ.take()
            tg = dma(SP, l_j[gjj], gj.rearrange("p b j t -> p b (j t)"),
                     scratch[:, :, g * 4:(g + 1) * 4, :].rearrange("b p j t -> p b (j t)"), t_g, gw, fz)
            return gj, gjj, tg

        def weighted(f, gj, j, ah, al, *after):
            fv = f.rearrange("p (b t) -> p b t", b=8)
            ta = tt(DV, fv, fv, gj[:, :, j, :], ALU.mult, *after)
            return ta, split(f, ah[:, j, :], al[:, j, :], ta, after)

        def neurons(g, st, js):
            if 0 in js:
                st["g"], st["a"] = weights_of(g), AA.take()
            (gj, gjj, tg), ((ah, al), aw, aj) = st["g"], st["a"]
            for j in js:
                wh, wl, wt, wj = slab("u", g * 4 + j)
                ps, pw, pj = PD.take()
                tp = dense_now(ps, by_slab(wh, wl), of_x(16, 528), wt, pw)
                done_with(wj, tp)
                f, fw, fj = AF.take()
                t1 = act(f, ps, ACT.Gelu, tp, fw)
                PD.give(pj, t1)
                ta, t2 = weighted(f, gj, j, ah, al, t1, tg, aw)
                AF.give(fj, t2)
            if 3 in js:
                GJ.give(gjj, ta)
            st["t"] = t2

        def fetched(g, st):
            fs, fw, fj = FS.take()
            tf = dma(SP, l_fs, fs, scratch2[4 * g:4 * g + 4].rearrange("j p t -> p j t"),
                     [spilled[4 * g + j] for j in range(4)], fw, fz)
            gj, gjj, tg = weights_of(g)
            (ah, al), aw, aj = st["a"] = AA.take()
            for j in range(4):
                ta, t2 = weighted(fs[:, j, :], gj, j, ah, al, tf, tg, aw)
            GJ.give(gjj, ta)
            FS.give(fj, t2)
            st["t"] = t2

        def back(g, st):
            (ah, al), _, aj = st["a"]
            ws = [slab("v", g * 4 + j) for j in range(4)]
            for db in range(8):
                ps, pw, pj = PA.take()
                terms = [x for j in range(4)
                         for x in terms3(ws[j][0][:, db, :], ws[j][1][:, db, :], ah[:, j, :], al[:, j, :])]
                tp = mm(ps, terms, [x[2] for x in ws], st["t"], pw)
                th = tt(DV, H[:, db, 16:528], H[:, db, 16:528], ps, ALU.add, tp)
                PA.give(pj, th)
            AA.give(aj, tp)
            for x in ws:
                done_with(x[3], tp)
            return th

        last = None
        for i in range(AHEAD):
            c, m = {}, {}
            neurons(AHEAD + i, c, (0, 1))
            if last is not None:
                back(AHEAD + i - 1, last)
            fetched(i, m)
            neurons(AHEAD + i, c, (2, 3))
            back(i, m)
            last = c
        t_h = back(31, last)
        dump("h2", H, t_h)

        fence()
        top[0] = base
        t_h = rmsnorm("final", [(16, 528)], t_h, None, dst=H)
        dump("h3", H, t_h)

        def expand(row, dst, nh, t):
            for d in range(2):
                t = tcopy(PO, dst[0:nh, :, d, :], row, t)
            return t

        def to_cols(src, nh, dst, t, full=None):
            ps, pw, pj = PA.take()
            for c in range(9):
                tp = mm(ps[:, c * nh:(c + 1) * nh], [(src[0:nh, c, :], IDENT[0:nh, 0:nh])], t, pw)
            v = ps[:, 0:9 * nh].rearrange("p (c h e) -> p c h e", c=9, e=2)
            r = []
            if dst is not None:
                for d in range(2):
                    lo = d * 64
                    r.append(copy(dst[lo:lo + 64, :, :], v[lo:lo + 64, :, :, d], tp))
            if full is not None:
                r.append(copy(full, ps[:, 0:9 * nh].rearrange("p (c h) -> p c h", c=9), tp))
            PA.give(pj, r)
            return r

        def row_bcast(row, h0, g, ps, *after):
            v = ps[:, 0:384].rearrange("p (c h i) -> p c h i", c=3, h=2)
            nh = row.shape[0]
            for d in range(2):
                tp = mm(v[:, :, d, :], [(IDENT[0:nh, h0 + d:h0 + d + 1].to_broadcast([nh, 128]), row[:, 3 * g:3 * g + 3, :])], *after)
            return tp

        def log_part(dst, y, tmp, nh, t, sign):
            t1 = act(tmp, y, ACT.Abs, t)
            t1 = act(tmp, tmp, ACT.Exp, t1, scale=-1.0)
            t1 = act(tmp, tmp, ACT.Ln, t1, bias=ONES[0:nh, 0:1])
            t2 = ts(DV, dst, y, sign, 0.0, ALU.mult, ALU.max, t)
            return tt(DV, dst, dst, tmp, ALU.add, t1, t2)

        def chunks(h0, c0):
            return [(0, 16, slice(0, 1), slice(48, 64)), (16, 272, slice(1, 5), slice(0, 64))] if c0 == 0 else \
                [(0, 256, slice(5, 9), slice(0, 64))]

        def ffn(layer):
            nonlocal t_h
            fence()
            top[0] = base
            t_x = rmsnorm(f"ffn{layer}", HALVES, t_h, PE.now())
            FH, FL = alloc2(16, 528)
            FT = Ring([alloc(272) for _ in range(4)])
            more_room((f"up{layer}", f"down{layer}"), 1, 2, [x.now() for x in ENGS])
            t_f = None
            for half in range(2):
                for fb in range(16):
                    wh, wl, wt, wj = slab(f"up{layer}", 16 * half + fb)
                    for a, b in HALVES:
                        ps, pw, pj = PD.take()
                        tp = dense_now(ps[:, 0:b - a], by_slab(wh, wl), of_x(a, b), wt, pw,
                                       by_k=lambda k: t_x(a, k))
                        f, fw, fj = FT.take()
                        f = f[:, 0:b - a]
                        t1 = act(f, ps[:, 0:b - a], ACT.Relu, tp, fw)
                        PD.give(pj, t1)
                        t1 = tt(DV, f, f, f, ALU.mult, t1)
                        ta = split(f, FH[:, fb, a:b], FL[:, fb, a:b], t1, t_f)
                        FT.give(fj, ta)
                    done_with(wj, tp)
                for fb in range(8):
                    ws = [slab(f"down{layer}", 4 * fb + 2 * half + q) for q in range(2)]
                    for a, b in HALVES:
                        ps, pw, pj = PA.take()
                        tp = dense_now(ps[:, 0:b - a],
                                       (lambda k: ws[k // 8][0][:, k % 8, :], lambda k: ws[k // 8][1][:, k % 8, :]),
                                       (lambda k: FH[:, k, a:b], lambda k: FL[:, k, a:b]),
                                       [x[2] for x in ws], pw, ta, n=16)
                        t_h = tt(DV, H[:, fb, a:b], H[:, fb, a:b], ps[:, 0:b - a], ALU.add, tp)
                        PA.give(pj, t_h)
                    for x in ws:
                        done_with(x[3], tp)
                t_f = tp

        def project_out(name, nk, OG, t_og):
            nonlocal t_h
            OH, OL = alloc2(8, 528)
            tp = None
            for q in range(nk // 8):
                for k in range(8):
                    ts_ = split(OG[:, 8 * q + k, 48:576], OH[:, k, :], OL[:, k, :], t_og, tp)
                for fb in range(8):
                    wh, wl, wt, wj = slab(name, (nk // 8) * fb + q)
                    for a, b in HALVES:
                        ps, pw, pj = PD.take()
                        tp = dense_now(ps[:, 0:b - a], by_slab(wh, wl),
                                       (lambda k: OH[:, k, a:b], lambda k: OL[:, k, a:b]), wt, pw, ts_)
                        t_h = tt(DV, H[:, fb, a:b], H[:, fb, a:b], ps[:, 0:b - a], ALU.add, tp)
                        PD.give(pj, t_h)
                    done_with(wj, tp)

        def small_proj(wt_ap, c0, nh, t):
            r = []
            for a, b in HALVES:
                ps, pw, pj = PA.take()
                tp = mm(ps[0:nh, 0:b - a], [(wt_ap[:, k, c0:c0 + nh], xs) for k in range(8)
                                            for xs in (XH[:, k, a:b].bitcast(F32), XL[:, k, a:b].bitcast(F32))],
                        pw, t, t_x(a))
                r.append((ps, pj, tp, a, b))
            return r

        t_x = rmsnorm("attn0", HALVES, [t_h, tx], PE.now())
        OG = alloc(16, 576)
        og_end = top[0]

        def phase_consts(nh, extra_w, ncol):
            w = alloc(8, ncol)
            t2 = dma(AC, once(), w, X[extra_w].rearrange("p (k f) -> p k f", k=8), [x.now() for x in ENGS])
            return w, t2

        RB = alloc(9, 64)[0:16]
        CUM = alloc(9, 64)[0:16]
        BC = alloc(9, 8)
        NBE = alloc(9, 8)
        CC = alloc(9, 8)
        LC = alloc(9, 8)
        LB = alloc(9, 16)
        work = top[0]
        BAW, t_sw = phase_consts(16, "w_ba", 32)
        RR = [alloc(9, 64)[0:16] for _ in range(3)]
        DUP = Ring([alloc(9, 2, 64)[0:16] for _ in range(2)])
        RST = alloc(576)[0:16]
        NA = alloc(2)
        t_rs = dma(AC, once(), RST, X["reset"][0:16, :])
        t_rs = [t_rs, t_sw]

        def flat_row(r):
            return r.rearrange("p c i -> p (c i)")

        def scan_rows(cum, g, nh, t):
            rst = RST[0:nh]
            return DV.do(lambda e: e.tensor_tensor_scan(flat_row(cum), rst, flat_row(g), 0.0, ALU.mult, ALU.add),
                         t, t_rs)

        def dup_cols(row, nh, dst, t, full=None):
            d, dw, dj = DUP.take()
            t1 = expand(row, d, nh, flat([t, dw]))
            r = to_cols(d.rearrange("p c d i -> p c (d i)"), nh, dst, t1, full)
            DUP.give(dj, r, PE.now())
            return r

        z0 = [mset(PO, RB, 0.0), mset(PO, RR[0], 0.0), mset(PO, RR[1], 0.0)]
        bt = []
        for ps, pj, tp, a, b in small_proj(BAW, 0, 16, t_sw):
            t1 = act(flat_row(RB)[:, 48 + a:48 + b], ps[0:16, 0:b - a], ACT.Sigmoid, tp, z0)
            PA.give(pj, t1)
            bt.append(t1)
        at = []
        for ps, pj, tp, a, b in small_proj(BAW, 16, 16, t_sw):
            t1 = act(flat_row(RR[0])[:, 48 + a:48 + b], ps[0:16, 0:b - a], ACT.Identity, tp, z0,
                     bias=ROWP[0:16, 1:2])
            PA.give(pj, t1)
            at.append(t1)
        t1 = act(NA[0:16, 0:1], ROWP[0:16, 0:1], ACT.Exp)
        t1 = ts(DV, NA[0:16, 1:2], NA[0:16, 0:1], -1.0, None, ALU.mult, None, t1)
        y = flat_row(RR[0])[:, 48:576]
        tmp = flat_row(RR[2])[:, 48:576]
        gsp = flat_row(RR[1])[:, 48:576]
        t2 = log_part(gsp, y, tmp, 16, [at, z0], 1.0)
        t2 = ts(DV, gsp, gsp, NA[0:16, 1:2], None, ALU.mult, None, t1, t2)
        t_cum = scan_rows(CUM, RR[1], 16, t2)
        t3 = tt(PO, RR[0], CUM[:, :, 63:64].to_broadcast([16, 9, 64]), CUM, ALU.subtract, t_cum, t2)
        tc1 = dup_cols(RB, 16, BC, bt)
        tc2 = dup_cols(CUM, 16, CC, t_cum)
        tc3 = dup_cols(RR[0], 16, LC, t3)
        t4 = tcopy(PO, RR[2], CUM[:, :, 63:64].to_broadcast([16, 9, 64]), t_cum, t2)
        tc4 = dup_cols(RR[2], 16, None, t4, LB)
        t5 = act(LC, LC, ACT.Exp, tc3)
        t5 = act(LB, LB, ACT.Exp, tc4)
        t5 = act(NBE, CC, ACT.Exp, tc2)
        t_cols = [t5, stt(NBE, NBE, -1.0, BC, ALU.mult, ALU.mult, t5, tc1)]
        fence()
        top[0] = work

        QD = Ring([alloc(9, 2, 64) for _ in range(2)])
        KD = Ring([alloc(9, 2, 64) for _ in range(2)])
        VD = Ring([alloc(9, 2, 64) for _ in range(2)])
        XC = Ring([alloc(532) for _ in range(1)])
        YC = Ring([alloc(528) for _ in range(1)])
        DD, BB, TA, TB, KE = (alloc(9, 128) for _ in range(5))
        MR = Ring([alloc(3, 128) for _ in range(3)])
        XR = Ring([alloc(3, 128) for _ in range(3)])
        RC = alloc(128)
        VN = alloc(128)
        ST = alloc(2, 128)
        z1 = [mset(PO, b, 0.0) for r in (QD, KD, VD) for b in r.bufs] + [mset(PO, OG, 0.0)]
        z1 = z1 + [mset(PO, b[:, 0:3], 0.0) for b in XC.bufs]
        state = {}

        def proj_gdn():
            for p in range(8):
                while not (QD.free and KD.free and VD.free):
                    yield 1
                st = {}
                qb, qw, qj = QD.take()
                kb, kw, kj = KD.take()
                vb, vw, vj = VD.take()
                for n in range(6):
                    wh, wl, wt, wj = slab("w_gdn", 6 * p + n)
                    if n < 4:
                        xc, xw, xj = XC.take()
                    toks = []
                    for a, b in HALVES:
                        ps, pw, pj = PD.take()
                        yield from dense(ps[:, 0:b - a], by_slab(wh, wl), of_x(a, b), wt, pw,
                                         by_k=lambda k: t_x(a, k))
                        tp = dense_tok[0]
                        if n < 4:
                            t1 = copy(xc[:, 3 + a:3 + b], ps[:, 0:b - a], tp, xw, z1)
                        else:
                            t1 = act(OG[:, 2 * p + n - 4, 48 + a:48 + b], ps[:, 0:b - a], ACT.Silu, tp, z1)
                        PD.give(pj, t1)
                        toks.append(t1)
                        yield 1
                    done_with(wj, tp)
                    if n < 4:
                        blk = [p, 8 + p, 16 + 2 * p, 17 + 2 * p][n]
                        yc, yw, yj = YC.take()
                        t2 = ts(DV, yc, xc[:, 3:531], col("conv", 4 * blk + 3), None, ALU.mult, None, toks, yw)
                        for s in (2, 1, 0):
                            t2 = stt(yc, xc[:, s:s + 528], col("conv", 4 * blk + s), yc, ALU.mult, ALU.add, t2)
                        XC.give(xj, t2)
                        if n >= 2:
                            t3 = act(vb[:, 0, n - 2, 48:64], yc[:, 0:16], ACT.Silu, t2, vw, z1)
                            t3 = act(vb[:, 1:9, n - 2, :], yc[:, 16:528].rearrange("p (c i) -> p c i", i=64),
                                     ACT.Silu, t2, vw, z1)
                            YC.give(yj, t3)
                            st["v"] = (vb, vj, t3)
                        else:
                            dst, dw, dj = (qb, qw, qj) if n == 0 else (kb, kw, kj)
                            t3 = act(yc, yc, ACT.Silu, t2)
                            yield 1
                            r, rw, rj = RT.take()
                            rt = []
                            for a, b in HALVES:
                                rt.append(inv_rms([yc[:, a:b]], b - a, 1.0, r[:, a:b], ONES, t3, rw))
                            sc = 128.0 ** -0.5 if n == 0 else 1.0
                            for d in range(2):
                                t4 = stt(dst[:, 0, d, 48:64], yc[:, 0:16], sc, r[:, 0:16], ALU.mult, ALU.mult,
                                         rt, dw, z1)
                                t4 = stt(dst[:, 1:9, d, :], yc[:, 16:528].rearrange("p (c i) -> p c i", i=64), sc,
                                         r[:, 16:528].rearrange("p (c i) -> p c i", i=64), ALU.mult, ALU.mult,
                                         rt, dw, z1)
                            YC.give(yj, t4)
                            RT.give(rj, t4)
                            st["qk"[n]] = (dst, dj, t4)
                    elif n == 5:
                        st["z"] = t1
                    yield 1
                state[p] = st

        t_og = []
        prev = {}

        def three(ap, g):
            return ap[:, 3 * g:3 * g + 3, :]

        def b3(c128):
            return c128.unsqueeze(1).to_broadcast([128, 3, 128])

        def decay(p, g, colsrc, rowtok, h0, rows, dd, ec, free):
            ps, pw, pj = PA.take()
            tp = row_bcast(rows, h0, g, ps, pw, rowtok)
            p3 = ps[:, 0:384].rearrange("p (c x) -> p c x", c=3)
            te = act(three(ec, g), p3, ACT.Exp, tp, free)
            t2 = tt(DV, three(dd, g), p3, colsrc[:, 3 * g:3 * g + 3, p:p + 1].to_broadcast([128, 3, 128]),
                    ALU.subtract, tp, te, free)
            PA.give(pj, t2)
            t2 = tt(PO, three(dd, g), three(dd, g), b3(CS["mask"]), ALU.add, t2)
            t2 = act(three(dd, g), three(dd, g), ACT.Exp, t2)
            return te, t2

        def pairs3(fn_l, fn_r, g, *after):
            ps, pw, pj = PA.take()
            for n in range(3):
                tp = mm(ps[:, n * 128:(n + 1) * 128], [(fn_l(3 * g + n, n), fn_r(3 * g + n, n))], pw, *after)
            return ps[:, 0:384].rearrange("p (c x) -> p c x", c=3), pj, tp

        def half3(lhs, rhs, g, *after):
            ps, pw, pj = PA.take()
            for n in range(3):
                tp = mm(ps[:, n * 64:n * 64 + 64], [(lhs[:, 3 * g + n, :], rhs[:, 3 * g + n, 0, :])], pw, *after)
            return (ps[:, 0:192].rearrange("p (c i) -> p c i", c=3).unsqueeze(2).to_broadcast([128, 3, 2, 64]),
                    pj, tp)

        def four(ap, g):
            return three(ap, g).rearrange("p c (h i) -> p c h i", h=2)

        def chain_gdn(p):
            st = state[p]
            (q, qj, tq), (k, kj, tk_), (v, vj, tv), tz = st["q"], st["k"], st["v"], st["z"]
            q2, k2, v2 = (x.rearrange("p c h i -> p c (h i)") for x in (q, k, v))
            free = prev.get("done")
            t_att, t_ec, t_ta, t_tb, t_bv, t_ke = {}, {}, {}, {}, {}, {}
            td, tb1 = {}, {}
            for g in range(3):
                te, td[g] = decay(p, g, CC, [t_cum, t_cols], 2 * p, CUM, DD, TA, free)
                t_ec[g] = te
                yield 2
            for g in range(3):
                psb, pbw, pbj = PA.take()
                tpb = row_bcast(RB, 2 * p, g, psb, pbw, bt)
                pk, pj, tp = half3(k2, k, g, tk_)
                t1 = tt(DV, four(BB, g), pk, four(DD, g), ALU.mult, tp, td[g], free)
                PA.give(pj, t1)
                tb1[g] = tt(DV, three(BB, g), psb[:, 0:384].rearrange("p (c x) -> p c x", c=3), three(BB, g),
                            ALU.mult, t1, tpb)
                PA.give(pbj, tb1[g])
                yield 2
                pk, pj, tp = half3(k2, q, g, tq)
                t_att[g] = tt(DV, four(DD, g), pk, four(DD, g), ALU.mult, tp, t1)
                PA.give(pj, t_att[g])
                t_ec[g] = tt(PO, three(q2, g), three(q2, g), three(TA, g), ALU.mult, tp, t_ec[g])
                ps, pw, pj = PA.take()
                for n in range(3):
                    tp = tr(ps[:, n * 128:(n + 1) * 128], v2[:, 3 * g + n, :], tv, pw)
                t_bv[g] = tt(DV, three(v2, g), ps[:, 0:384].rearrange("p (c x) -> p c x", c=3),
                             BC[:, 3 * g:3 * g + 3, p:p + 1].to_broadcast([128, 3, 128]), ALU.mult, tp)
                PA.give(pj, t_bv[g])
                yield 2
            ms = {}
            for g in range(3):
                ps, pw, pj = PA.take()
                for n in range(3):
                    tp = tr(ps[:, n * 128:(n + 1) * 128], k2[:, 3 * g + n, :], tk_, pw)
                t_ke[g] = tt(DV, three(KE, g), ps[:, 0:384].rearrange("p (c x) -> p c x", c=3),
                             LC[:, 3 * g:3 * g + 3, p:p + 1].to_broadcast([128, 3, 128]), ALU.mult, tp, free)
                PA.give(pj, t_ke[g])
                m, mw, mj = MR.take()
                tm_ = tt(PO, m, three(BB, g), b3(CS["lev0"]), ALU.mult, tb1[g], mw)
                t_tb[g] = tt(PO, three(TB, g), b3(IDENT), m, ALU.subtract, tm_, free)
                ms[g] = (m, mj, tm_)
                yield 1
            for g in range(3):
                m, mj, tm_ = ms[g]
                ps, pw, pj = PA.take()
                for n in range(3):
                    tp = tr(ps[:, n * 128:(n + 1) * 128], m[:, n, :], tm_, pw)
                px = ps[:, 0:384].rearrange("p (c x) -> p c x", c=3)
                t_ta[g] = tt(DV, three(TA, g), b3(IDENT), px, ALU.subtract, tp, t_ec[g])
                PA.give(pj, t_ta[g])
                MR.give(mj, t_tb[g], tp)
                yield 1
            for lv in range(1, 6):
                xs = {}
                for g in range(3):
                    m, mw, mj = MR.take()
                    tm_ = tt(PO, m, three(BB, g), b3(CS[f"lev{lv}"]), ALU.mult, mw)
                    px, pj, tp = pairs3(lambda c, n: m[:, n, :], lambda c, n: TA[:, c, :], g, tm_, t_ta[g])
                    MR.give(mj, tp)
                    x, xw, xj = XR.take()
                    tx_ = copy(x, px, tp, xw)
                    PA.give(pj, tx_)
                    xs[g] = (x, xj, tx_)
                    yield 1
                b = 1 << lv

                def cols(ap, o):
                    return ap.rearrange("p (m r) -> p m r", r=2 * b)[:, :, o:o + b]

                def part(lhs, rhs, o, g, *after):
                    ps, pw, pj = PA.take()
                    for n in range(3):
                        tp = mm(ps[:, n * 64:n * 64 + 64].rearrange("p (m r) -> p m r", r=b),
                                [(lhs(n), cols(rhs(n), o))], pw, *after)
                    return ps[:, 0:192].rearrange("p (m r) -> p m r", r=b), pj, tp

                for g in range(3):
                    x, xj, tx_ = xs[g]
                    ta3 = three(TA, g).rearrange("p c x -> p (c x)")
                    tb3 = three(TB, g).rearrange("p c x -> p (c x)")
                    if lv < 5:
                        pd, pdj, tpd = part(lambda n: TB[:, 3 * g + n, :], lambda n: x[:, n, :], 0, g, tx_, t_tb[g])
                        t_ta[g] = tt(DV, cols(ta3, 0), cols(ta3, 0), pd, ALU.subtract, tpd)
                        PA.give(pdj, t_ta[g])
                    pt, ptj, tpt = part(lambda n: x[:, n, :], lambda n: TB[:, 3 * g + n, :], b, g, tx_, t_tb[g])
                    XR.give(xj, tpt)
                    t_tb[g] = tt(DV, cols(tb3, b), cols(tb3, b), pt, ALU.subtract, tpt)
                    PA.give(ptj, t_tb[g])
                    yield 1
            t_s = mset(PO, ST, 0.0, free)
            t_r = t_v = None
            for c in range(9):
                g = c // 3
                ps, pw, pj = PA.take()
                for d in range(2):
                    tp = mm(ps[d * 64:d * 64 + 64, 0:128], [(k[:, c, d, :], ST[:, d, :])], t_s, pw)
                t_r = stt(RC, ps[:, 0:128], NBE[:, c, p:p + 1], v2[:, c, :], ALU.mult, ALU.add, tp, t_bv[g], t_v)
                PA.give(pj, t_r)
                yield 2
                ps, pw, pj = PA.take()
                tp = mm(ps[:, 0:128], [(TB[:, c, :], RC)], t_r, t_tb[g], pw)
                t_v = copy(VN, ps[:, 0:128], tp, PE.now())
                PA.give(pj, t_v)
                yield 2
                news = []
                po, pow_, poj = PA.take()
                mm(po[:, 0:128], [(VN, DD[:, c, :])], pow_, t_v, t_att[g], t_ec[g], stop=False)
                for d in range(2):
                    tp = mm(po[:, d * 64:d * 64 + 64], [(ST[:, d, :], q2[:, c, d * 64:d * 64 + 64])],
                            start=False, stop=d == 1)
                for d in range(2):
                    ps, pw, pj = PA.take()
                    tps = mm(ps[:, 0:128], [(KE[d * 64:d * 64 + 64, c, :], VN[d * 64:d * 64 + 64, :])], pw, t_ke[g])
                    news.append((ps, pj, tps))
                t_o = copy(v2[:, c, :], po[:, 0:128], tp)
                PA.give(poj, t_o)
                t_s = []
                for d, (ps, pj, tps) in enumerate(news):
                    t = stt(ST[:, d, :], ST[:, d, :], LB[:, c, 2 * p + d:2 * p + d + 1], ps[:, 0:128],
                            ALU.mult, ALU.add, tps, tp)
                    PA.give(pj, t)
                    t_s.append(t)
                yield 2
            done = [t_s, t_o, PE.now()]
            QD.give(qj, done, [t_ec[g] for g in range(3)])
            KD.give(kj, done)
            og = OG[:, 2 * p:2 * p + 2, :].rearrange("p h (c i) -> p c h i", c=9)
            for g in range(3):
                r, rw, rj = RT.take()
                r3 = r[:, 0:384].rearrange("p (c x) -> p c x", c=3)
                t1 = inv_rms([three(v2, g)], 384, 1.0 / 128, r[:, 0:384], ONES, t_o, rw, ring=PA)
                t0 = t1
                t1 = [tt(PO, r3[:, :, d * 64:d * 64 + 64], r3[:, :, d * 64:d * 64 + 64],
                         og[:, 3 * g:3 * g + 3, d, :], ALU.mult, t0, tz) for d in range(2)]
                for d in range(2):
                    t2 = stt(og[:, 3 * g:3 * g + 3, d, :], v[:, 3 * g:3 * g + 3, d, :], col("gdnn"),
                             r3[:, :, d * 64:d * 64 + 64], ALU.mult, ALU.mult, t1)
                RT.give(rj, t2)
                yield 1
            VD.give(vj, t2)
            t_og.append(t2)
            prev["done"] = [done, [x.now() for x in ENGS]]

        def chain_all(chain, n):
            for p in range(n):
                while p not in state:
                    yield 1
                yield from chain(p)

        weave(proj_gdn(), chain_all(chain_gdn, 8))
        fence()
        top[0] = og_end
        project_out("gdn_out", 16, OG, t_og[-1])
        dump("h4", H, t_h)
        ffn(0)
        dump("h5", H, t_h)

        fence()
        top[0] = base
        t_x = rmsnorm("attn1", HALVES, t_h, PE.now())
        OG = alloc(8, 576)
        og_end = top[0]
        GWT, t_sw = phase_consts(8, "w_if", 16)
        IR = alloc(9, 64)[0:8]
        CUM = alloc(9, 64)[0:8]
        CC, LC, LB = alloc(9, 4), alloc(9, 4), alloc(9, 4)
        work = top[0]
        RR = [alloc(9, 64)[0:16] for _ in range(3)]
        RR8 = [x[0:8] for x in RR]
        DUP = Ring([alloc(9, 2, 64)[0:16] for _ in range(2)])
        RST = alloc(576)[0:16]
        GBI = alloc(2)
        t_rs = dma(AC, once(), RST, X["reset"][0:16, :])
        t_rs = [t_rs, t_sw]
        tg = ts(DV, GBI[0:8, :], ROWP[0:8, 2:4], 1.0 / 15.0, None, ALU.mult, None)
        z0 = [mset(PO, IR, 0.0), mset(PO, RR[0], 0.0), mset(PO, RR[1], 0.0)]
        ab = []
        for n, dst in ((0, IR), (1, RR8[0])):
            for ps, pj, tp, a, b in small_proj(GWT, 8 * n, 8, t_sw):
                dv = flat_row(dst)[:, 48 + a:48 + b]
                t1 = act(dv, ps[0:8, 0:b - a], ACT.Tanh, tp, z0, tg, bias=GBI[0:8, n:n + 1], scale=1.0 / 15.0)
                PA.give(pj, t1)
                ab.append(ts(DV, dv, dv, 15.0, None, ALU.mult, None, t1))
        y = flat_row(RR8[0])[:, 48:576]
        lf = flat_row(RR8[1])[:, 48:576]
        t2 = log_part(lf, y, flat_row(RR8[2])[:, 48:576], 8, [ab, z0], -1.0)
        t2 = ts(DV, lf, lf, -1.0, None, ALU.mult, None, t2)
        t_cum = scan_rows(CUM, RR8[1], 8, t2)
        t3 = tt(PO, RR8[0], CUM, IR, ALU.subtract, t_cum, ab, t2)
        tc1 = dup_cols(RR8[0], 8, CC, t3)
        t4 = tt(PO, RR8[2], CUM[:, :, 63:64].to_broadcast([8, 9, 64]), RR8[0], ALU.subtract, t3, t2)
        tc2 = dup_cols(RR8[2], 8, LC, t4)
        t4 = tcopy(PO, RR8[1], CUM[:, :, 63:64].to_broadcast([8, 9, 64]), t_cum)
        tc3 = dup_cols(RR8[1], 8, LB, t4)
        t5 = act(LC, LC, ACT.Exp, tc2)
        t_cols = [act(LB, LB, ACT.Exp, tc3, t5), tc1]
        fence()
        top[0] = work

        QD = Ring([alloc(9, 2, 64) for _ in range(2)])
        KD = Ring([alloc(9, 2, 64) for _ in range(2)])
        VD = Ring([alloc(9, 2, 64) for _ in range(2)])
        EC, DD, BV, KE, DEN = (alloc(9, 128) for _ in range(5))
        ST = alloc(256)
        z1 = [mset(PO, b, 0.0) for r in (QD, KD, VD) for b in r.bufs] + [mset(PO, OG, 0.0)]
        state.clear()
        prev.clear()
        t_og = []

        def proj_ml():
            for p in range(4):
                while not (QD.free and KD.free and VD.free):
                    yield 1
                st = {}
                bufs = [QD.take(), KD.take(), VD.take()]
                for n in range(6):
                    wh, wl, wt, wj = slab("w_ml", 6 * p + n)
                    for hf, (a, b) in enumerate(HALVES):
                        ps, pw, pj = PD.take()
                        yield from dense(ps[:, 0:b - a], by_slab(wh, wl), of_x(a, b), wt, pw,
                                         by_k=lambda k: t_x(a, k))
                        tp = dense_tok[0]
                        if n >= 4:
                            ts_ = act(OG[:, 2 * p + n - 4, 48 + a:48 + b], ps[:, 0:b - a], ACT.Sigmoid, tp, z1)
                            st["z"] = ts_
                        else:
                            buf, bw, bj = bufs[[0, 1, 2, 2][n]]
                            ts_ = []
                            for lo, hi, cs, is_ in chunks(0, hf):
                                wd = is_.stop - is_.start
                                if n < 2:
                                    for d in range(2):
                                        pp = slice(d * 64, d * 64 + 64)
                                        ts_.append(act(buf[pp, cs, d, is_],
                                                       ps[pp, lo:hi].rearrange("p (c i) -> p c i", i=wd),
                                                       ACT.Copy, tp, bw, z1, scale=1.0 if n == 0 else 0.125))
                                else:
                                    ts_.append(copy(buf[:, cs, n % 2, is_],
                                                    ps[:, lo:hi].rearrange("p (c i) -> p c i", i=wd), tp, bw, z1))
                            st["qkvv"[n]] = (buf, bj, ts_[-1])
                        PD.give(pj, ts_)
                        yield 1
                    done_with(wj, tp)
                state[p] = st

        def chain_ml(p):
            st = state[p]
            (q, qj, tq), (k, kj, tk_), (v, vj, tv), tz = st["q"], st["k"], st["v"], st["z"]
            q2, k2, v2 = (x.rearrange("p c h i -> p c (h i)") for x in (q, k, v))
            free = prev.get("done")
            t_w, t_ec, t_bv, t_ke = {}, {}, {}, {}
            for g in range(3):
                te, td = decay(p, g, CC, [t_cum, t_cols], 2 * p, CUM, DD, EC, free)
                t_ec[g] = tt(PO, three(EC, g), three(EC, g), three(q2, g), ALU.mult, te, tq)
                yield 2
                pk, pj, tp = pairs3(lambda c, n: k2[:, c, :], lambda c, n: q2[:, c, :], g, tq, tk_)
                t_w[g] = tt(DV, three(DD, g), pk, three(DD, g), ALU.mult, tp, td)
                PA.give(pj, t_w[g])
                ps, pw, pj = PA.take()
                for n in range(3):
                    tp = tr(ps[:, n * 128:(n + 1) * 128], v2[:, 3 * g + n, :], tv, pw)
                t_bv[g] = copy(three(BV, g), ps[:, 0:384].rearrange("p (c x) -> p c x", c=3), tp, free)
                PA.give(pj, t_bv[g])
                ps, pw, pj = PA.take()
                for n in range(3):
                    tp = tr(ps[:, n * 128:(n + 1) * 128], k2[:, 3 * g + n, :], tk_, pw)
                t_ke[g] = tt(DV, three(KE, g), ps[:, 0:384].rearrange("p (c x) -> p c x", c=3),
                             LC[:, 3 * g:3 * g + 3, p:p + 1].to_broadcast([128, 3, 128]), ALU.mult, tp, free)
                PA.give(pj, t_ke[g])
                yield 2
            t_s = mset(PO, ST, 0.0, free)
            for c in range(9):
                g = c // 3
                ps, pw, pj = PA.take()
                tp = mm(ps[:, 0:128], [(BV[:, c, :], DD[:, c, :]), (ST[:, 0:128], EC[:, c, :])],
                        pw, t_s, t_w[g], t_ec[g], t_bv[g])
                tp = mm(ps[:, 128:256], [(ONES, DD[:, c, :]), (ST[:, 128:256], EC[:, c, :])])
                t_n = copy(v2[:, c, :], ps[:, 0:128], tp)
                t_d = act(DEN[:, c, :], ps[:, 128:256], ACT.Abs, tp, free)
                PA.give(pj, t_n, t_d)
                ps, pw, pj = PA.take()
                mm(ps[:, 0:128], [(KE[:, c, :], BV[:, c, :])], pw, t_ke[g])
                tp = mm(ps[:, 128:256], [(KE[:, c, :], ONES)])
                t_s = stt(ST, ST, LB[:, c, p:p + 1], ps[:, 0:256], ALU.mult, ALU.add, tp, t_s)
                PA.give(pj, t_s)
                yield 4
            done = [t_s, PE.now()]
            QD.give(qj, done, [t_ec[g] for g in range(3)])
            KD.give(kj, done)
            og = OG[:, 2 * p:2 * p + 2, :].rearrange("p h (c i) -> p c h i", c=9)
            for g in range(3):
                t1 = ts(DV, three(DEN, g), three(DEN, g), 1.0, None, ALU.max, None, t_d)
                t1 = recip(three(DEN, g), three(DEN, g), t1)
                t1 = tt(DV, three(v2, g), three(v2, g), three(DEN, g), ALU.mult, t1, t_n)
                r, rw, rj = RT.take()
                r3 = r[:, 0:384].rearrange("p (c x) -> p c x", c=3)
                t1 = inv_rms([three(v2, g)], 384, 1.0 / 128, r[:, 0:384], ONES, t1, rw, ring=PA)
                t0 = t1
                t1 = [tt(PO, r3[:, :, d * 64:d * 64 + 64], r3[:, :, d * 64:d * 64 + 64],
                         og[:, 3 * g:3 * g + 3, d, :], ALU.mult, t0, tz) for d in range(2)]
                for d in range(2):
                    t2 = stt(og[:, 3 * g:3 * g + 3, d, :], v[:, 3 * g:3 * g + 3, d, :], col("mln", 2 * p + d),
                             r3[:, :, d * 64:d * 64 + 64], ALU.mult, ALU.mult, t1)
                RT.give(rj, t2)
                yield 1
            VD.give(vj, t2)
            t_og.append(t2)
            prev["done"] = [done, [x.now() for x in ENGS]]

        weave(proj_ml(), chain_all(chain_ml, 4))
        fence()
        top[0] = og_end
        project_out("ml_out", 8, OG, t_og[-1])
        dump("h6", H, t_h)
        ffn(1)
        l_o = Line(sem("s_o"))
        to = dma(SP, l_o, out.rearrange("p (k t) -> p k t", k=8), H[:, :, 16:528], t_h)
        SP.items.append((flat([to, t_g, list(spilled.values()), (l_dbg.sem, l_dbg.n) if l_dbg.n else None]), None, None, 0))

        print("items", [len(e.items) for e in (PE, DV, AC, PO, SP)], [e.n for e in (PE, DV, AC, PO)])
        block = ctx.enter_context(nc.Block())
        block.sync(SP.play)
        block.tensor(PE.play)
        block.vector(DV.play)
        block.scalar(AC.play)
        block.gpsimd(PO.play)


def kernel(**inputs):
    import concourse.bacc as bacc
    from concourse.bass_utils import run_bass_kernel_spmd as run

    I = {k: np.asarray(v) for k, v in inputs.items()}

    def c(a):
        return np.ascontiguousarray(a)

    def slabs(w):
        K, F = w.shape
        return c(w.reshape(K // 1024, 8, 128, F // 128, 128).transpose(3, 0, 2, 1, 4)).reshape(-1, 128, 1024)

    def colv(v):
        return v.reshape(-1, 128).T

    arr = {}
    cs = consts()
    arr["cst"] = c(np.concatenate([cs[n] for n in CONST_SMALL], axis=1))
    arr["negdist"] = cs["negdist"]
    arr["reset"] = c(cs["reset"])
    conv = I["gdn_conv_2"][0]
    arr["cols"] = c(np.concatenate([
        colv(I["norm1_w"][0]), colv(I["norm2_w"][0]), colv(I["final_norm_w"]), colv(I["attn_norm_2"][0]),
        colv(I["attn_norm_2"][1]), colv(I["ffn_norm_2"][0]), colv(I["ffn_norm_2"][1]), colv(I["b_gate"][0]),
        conv.reshape(4, 32, 128).transpose(2, 1, 0).reshape(128, 128), colv(I["gdn_norm_2"][0]),
        colv(I["mlstm_norm_2"][0]), colv(I["diff_subln_w"][0])], axis=1))
    gb = I["mlstm_gate_bias_2"][0]
    rows = np.zeros((16, 4), np.float32)
    rows[:, 0], rows[:, 1] = I["gdn_a_log_2"][0], I["gdn_dt_bias_2"][0]
    rows[0:8, 2], rows[0:8, 3] = gb[0:8], gb[8:16]
    arr["rows"] = rows
    arr["x"] = c(I["x"][0].reshape(512, 8, 128).transpose(2, 1, 0)).reshape(128, 4096)
    arr["meta"] = c(I["meta_tokens_2"].reshape(16, 8, 128).transpose(2, 1, 0)).reshape(128, 128)
    rel = np.clip(np.arange(128)[:, None] - (np.arange(512)[None, :] - 384), -128, 128) + 128
    arr["bias"] = c(I["chunk_rel_bias"][0][:, rel].transpose(1, 0, 2)).reshape(128, 4096)
    lq = np.stack([I["diff_lq1"][0], I["diff_lk1"][0], I["diff_lq2"][0], I["diff_lk2"][0]])
    arr["lq"] = c(np.broadcast_to(lq.reshape(1, 256), (128, 256)))
    w = slabs(I["w_in"][0])
    order = [x for h in range(8) for x in (h, 8 + h, 16 + h)] + [x for h in range(4) for x in (24 + h, 28 + h, 32 + h)]
    arr["w_att"] = w[order]
    arr["w_gate"] = w[[x for f in range(8) for x in (36 + f, 44 + f)]]
    arr["w_bd"] = slabs(I["w_branch_diff"][0])
    arr["w_bc"] = c(I["w_branch_chunk"][0].reshape(4, 128, 4, 2, 128).transpose(2, 1, 3, 0, 4)).reshape(4, 128, 1024)
    arr["w_out"] = slabs(I["w_out"][0])
    arr["w_q"] = slabs(I["peer_wq"][0])
    arr["keys"] = c(I["peer_keys"][0].transpose(1, 3, 0, 2)).reshape(128, 1024)
    arr["u"] = c(I["peer_u"][0].reshape(128, 128, 8, 128).transpose(1, 3, 2, 0)).reshape(128, 128, 1024)
    arr["v"] = c(I["peer_v"][0].reshape(128, 128, 1024).transpose(1, 0, 2))
    g = I["gdn_in_2"][0]
    wg = slabs(g[:, 0:6144])
    arr["w_gdn"] = wg[[x for p in range(8) for x in (p, 8 + p, 16 + 2 * p, 17 + 2 * p, 32 + 2 * p, 33 + 2 * p)]]
    arr["w_ba"] = c(g[:, 6144:6176].reshape(8, 128, 32).transpose(1, 0, 2)).reshape(128, 256)
    arr["gdn_out"] = slabs(I["gdn_out_2"][0])
    m = I["mlstm_in_2"][0]
    wm = slabs(m[:, 0:3072])
    arr["w_ml"] = wm[[x for p in range(4) for x in (p, 4 + p, 8 + 2 * p, 9 + 2 * p, 16 + 2 * p, 17 + 2 * p)]]
    arr["w_if"] = c(m[:, 3072:3088].reshape(8, 128, 16).transpose(1, 0, 2)).reshape(128, 128)
    arr["ml_out"] = slabs(I["mlstm_out_2"][0])
    for l in range(2):
        arr[f"up{l}"] = slabs(I["ff_up_2"][l])
        arr[f"down{l}"] = slabs(I["ff_down_2"][l])

    nc = bacc.Bacc("TRN2", target_bir_lowering=False, num_devices=1)
    X = {n: nc.dram_tensor("in_" + n, a.shape, F32, kind="ExternalInput").ap() for n, a in arr.items()}
    out = nc.dram_tensor("out_0", (128, 4096), F32, kind="ExternalOutput").ap()
    scratch = nc.dram_tensor("scratch", (8, 128, 128, 64), F32, kind="Internal").ap()
    scratch2 = nc.dram_tensor("scratch2", (4 * AHEAD, 128, 512), F32, kind="Internal").ap()
    dbg = {n: nc.dram_tensor("dbg_" + n, (128,) + s, F32, kind="ExternalOutput").ap() for n, s in DBG}
    build(nc, X, out, scratch, scratch2, dbg)
    r = run(nc, [{"in_" + n: a for n, a in arr.items()}], core_ids=[0])
    got = r.results[0]["out_0"]
    return c(got.reshape(128, 8, 512).transpose(2, 1, 0)).reshape(1, 512, 1024)
```
